# Optimizing a Trainium2 kernel written in Bass

```python
import numpy as np
import jax
import jax.numpy as jnp
from jax import lax

D_MODEL = 2048
BATCH = 1
SEQ = 512
DEPTH = 1
DEC_BATCH = 8
DEC_SEQ = 1
PAST_LEN = 4096
PAGE_SIZE = 128

D_HG = D_MODEL // 2
D_NSA = D_MODEL - D_HG
HG_DK = 128
HG_DV = 128
HG_HEADS = D_HG // HG_DK
HG_CHUNK = 32
NSA_DH = 64
NSA_HEADS = D_NSA // NSA_DH
NSA_KV_HEADS = 4
NSA_GROUP = NSA_HEADS // NSA_KV_HEADS
KV_DIM = NSA_KV_HEADS * NSA_DH
CMP_L = 32
CMP_D = 16
CMP_R = CMP_L // CMP_D
CMP_HID = 2 * NSA_DH
SLC_L = 64
N_SEL = 16
WINDOW = 512
SLC_QBLK = 16
WIN_QBLK = 128
D_IN = 4 * D_HG + 2 * D_NSA + 6 * KV_DIM + 3 * NSA_HEADS
ALPHA = (2.0 * DEPTH) ** 0.25
BETA = (8.0 * DEPTH) ** -0.25
LN_EPS = 1e-5
RMS_EPS = 1e-6
FORCED_SCORE = 1e4

kernel_name = 'hymba_hgrn2_nsa_decode_step'

def masked_softmax(s, mask, axes):
    s = jnp.where(mask, s.astype(jnp.float32), -jnp.inf)
    m = jnp.max(s, axis=axes, keepdims=True)
    m = jnp.where(jnp.isfinite(m), m, 0.0)
    p = jnp.exp(s - m)
    den = jnp.sum(p, axis=axes, keepdims=True)
    return p / jnp.where(den > 0, den, 1.0)

def split_proj(x, w_in):
    h = jnp.einsum('btd,de->bte', x, w_in)
    sizes = [D_HG] * 4 + [D_NSA, 6 * KV_DIM, 3 * NSA_HEADS, D_NSA]
    offs = np.cumsum(sizes)[:-1].tolist()
    return jnp.split(h, offs, axis=-1)

def hgrn2_chunk(S, inp):
    q, k, v, logf = inp
    C = q.shape[1]
    A = jnp.cumsum(logf, axis=1)
    causal = jnp.tril(jnp.ones((C, C), dtype=bool))[None, :, :, None, None]
    decay = jnp.exp(jnp.where(causal, A[:, :, None] - A[:, None, :], -jnp.inf))
    attn = jnp.einsum('bthk,btshk,bshk->bhts', q, decay, k)
    o = jnp.einsum('bhts,bshv->bthv', attn, v) + jnp.einsum('bthk,bhkv->bthv', q * jnp.exp(A), S)
    a_last = A[:, -1]
    S = S * jnp.exp(a_last)[..., None] + jnp.einsum('bshk,bshv->bhkv', k * jnp.exp(a_last[:, None] - A), v)
    return S, o

def hgrn2_mix(hq, hf, hi, hgate, S0, lb, norm_g):
    B, T, _ = hq.shape
    f_raw = hf.astype(jnp.float32)
    logf = jnp.log(lb + (1.0 - lb) * jax.nn.sigmoid(f_raw))
    k = (1.0 - lb) * jax.nn.sigmoid(-f_raw)
    q = hq.astype(jnp.float32)
    v = hi.astype(jnp.float32)
    C = HG_CHUNK if T % HG_CHUNK == 0 else T
    n = T // C

    def to_chunks(a, d):
        return jnp.moveaxis(a.reshape(B, n, C, HG_HEADS, d), 1, 0)

    S, o = lax.scan(hgrn2_chunk, S0.astype(jnp.float32),
                    (to_chunks(q, HG_DK), to_chunks(k, HG_DK), to_chunks(v, HG_DV), to_chunks(logf, HG_DK)))
    o = jnp.moveaxis(o, 0, 1).reshape(B, T, HG_HEADS, HG_DV)
    o = o * lax.rsqrt(jnp.mean(o * o, axis=-1, keepdims=True) + RMS_EPS)
    o = o.reshape(B, T, D_HG) * norm_g * jax.nn.silu(hgate.astype(jnp.float32))
    return o, S

def compress(rows, w1, w2, pe):
    B, T = rows.shape[:2]
    n_sub = T // CMP_D
    n_cmp = n_sub - CMP_R + 1
    sub = rows[:, :n_sub * CMP_D].reshape(B, n_sub, CMP_D, NSA_KV_HEADS, NSA_DH)
    proj = jnp.einsum('bnjhd,rjde->rbnhe', sub, w1.reshape(CMP_R, CMP_D, NSA_DH, CMP_HID))
    h = jnp.einsum('jd,jde->e', pe, w1)
    for r in range(CMP_R):
        h = h + proj[r, :, r:r + n_cmp]
    return jnp.einsum('bnhe,ed->bnhd', jax.nn.silu(h), w2)

def cmp_attention(q, kc, vc, qpos):
    n_cmp = kc.shape[1]
    end = jnp.arange(n_cmp) * CMP_D + CMP_L - 1
    s = jnp.einsum('bqhgd,bnhd->bqhgn', q, kc) * NSA_DH ** -0.5
    mask = (end[None, :] <= qpos[:, None])[None, :, None, None, :]
    p = masked_softmax(s, mask, -1)
    return jnp.einsum('bqhgn,bnhd->bqhgd', p, vc), p

def select_blocks(p, qpos, n_slc):
    n_cmp = p.shape[-1]
    ci = np.arange(n_cmp)[:, None] * CMP_D
    sj = np.arange(n_slc)[None, :] * SLC_L
    overlap = jnp.asarray(((ci < sj + SLC_L) & (ci + CMP_L > sj)).astype(np.float32))
    imp = jnp.einsum('bqhn,nj->bqhj', p.sum(axis=3), overlap)
    jb = jnp.arange(n_slc)[None, :]
    cur = (qpos // SLC_L)[:, None]
    forced = (jb == 0) | (jb == cur) | (jb == cur - 1)
    valid = jb * SLC_L <= qpos[:, None]
    score = jnp.where(forced[None, :, None, :], FORCED_SCORE, jnp.where(valid[None, :, None, :], imp, -1.0))
    _, sel = lax.top_k(score, min(N_SEL, n_slc))
    return sel

def to_blocks(rows):
    B, T = rows.shape[:2]
    n_slc = -(-T // SLC_L)
    rows = jnp.pad(rows, ((0, 0), (0, n_slc * SLC_L - T), (0, 0), (0, 0)))
    return rows.reshape(B, n_slc, SLC_L, NSA_KV_HEADS, NSA_DH).transpose(0, 3, 1, 2, 4)

def selected_attention(q, kb, vb, sel, qpos):
    B = q.shape[0]
    bi = jnp.arange(B)[:, None, None, None]
    hi = jnp.arange(NSA_KV_HEADS)[None, None, :, None]
    kg = kb[bi, hi, sel]
    vg = vb[bi, hi, sel]
    s = jnp.einsum('bqhgd,bqhkld->bqhgkl', q, kg) * NSA_DH ** -0.5
    kpos = sel[..., None] * SLC_L + jnp.arange(SLC_L)
    mask = (kpos <= qpos[None, :, None, None, None])[:, :, :, None]
    p = masked_softmax(s, mask, (-2, -1))
    return jnp.einsum('bqhgkl,bqhkld->bqhgd', p, vg)

def window_attention(q, k, v, qpos, kpos):
    s = jnp.einsum('bqhgd,bkhd->bqhgk', q, k) * NSA_DH ** -0.5
    rel = qpos[:, None] - kpos[None, :]
    mask = ((rel >= 0) & (rel < WINDOW) & (kpos[None, :] >= 0))[None, :, None, None, :]
    p = masked_softmax(s, mask, -1)
    return jnp.einsum('bqhgk,bkhd->bqhgd', p, v)

def blocked_over_queries(fn, T, blk):
    out = lax.map(fn, jnp.arange(T // blk))
    return jnp.moveaxis(out, 0, 1).reshape((out.shape[1], T) + out.shape[3:])

def nsa_cmp_slc(q, rows, qpos, cmp_w1, cmp_w2, cmp_pe, blocked):
    kc = compress(rows[:, :, 0], cmp_w1[0], cmp_w2[0], cmp_pe[0])
    vc = compress(rows[:, :, 1], cmp_w1[1], cmp_w2[1], cmp_pe[1])
    o_cmp, p = cmp_attention(q, kc, vc, qpos)
    kb = to_blocks(rows[:, :, 2])
    vb = to_blocks(rows[:, :, 3])
    sel = select_blocks(p, qpos, kb.shape[2])
    if blocked:
        def one(j):
            st = j * SLC_QBLK
            return selected_attention(lax.dynamic_slice_in_dim(q, st, SLC_QBLK, 1), kb, vb,
                                      lax.dynamic_slice_in_dim(sel, st, SLC_QBLK, 1),
                                      lax.dynamic_slice_in_dim(qpos, st, SLC_QBLK, 0))
        o_slc = blocked_over_queries(one, q.shape[1], SLC_QBLK)
    else:
        o_slc = selected_attention(q, kb, vb, sel, qpos)
    return o_cmp, o_slc

def nsa_combine(o_cmp, o_slc, o_win, ngates, ngate):
    B, T = ngates.shape[:2]
    g = jax.nn.sigmoid(ngates.astype(jnp.float32)).reshape(B, T, 3, NSA_KV_HEADS, NSA_GROUP)[..., None]
    o = g[:, :, 0] * o_cmp + g[:, :, 1] * o_slc + g[:, :, 2] * o_win
    return o.reshape(B, T, D_NSA) * jax.nn.silu(ngate.astype(jnp.float32))

def post_norm(x, o_hg, o_nsa, w_out, ln_g, ln_b):
    y = jnp.einsum('bte,ed->btd', jnp.concatenate([o_hg, o_nsa], axis=-1), w_out)
    z = ALPHA * x.astype(jnp.float32) + y
    mu = jnp.mean(z, axis=-1, keepdims=True)
    var = jnp.mean(jnp.square(z - mu), axis=-1, keepdims=True)
    return ((z - mu) * lax.rsqrt(var + LN_EPS) * ln_g + ln_b).astype(x.dtype)

def prompt_layer(x, w_in, lb, hg_norm_g, cmp_w1, cmp_w2, cmp_pe, w_out, ln_g, ln_b):
    B, T, _ = x.shape
    hq, hf, hi, hgate, nq, kv, ngates, ngate = split_proj(x, w_in)
    S0 = jnp.zeros((B, HG_HEADS, HG_DK, HG_DV), jnp.float32)
    o_hg, S = hgrn2_mix(hq, hf, hi, hgate, S0, lb, hg_norm_g)
    q = nq.reshape(B, T, NSA_KV_HEADS, NSA_GROUP, NSA_DH)
    kv = kv.reshape(B, T, 6, NSA_KV_HEADS, NSA_DH)
    rows, win = kv[:, :, :4], kv[:, :, 4:]
    qpos = jnp.arange(T)
    o_cmp, o_slc = nsa_cmp_slc(q, rows, qpos, cmp_w1, cmp_w2, cmp_pe, True)
    win_pad = jnp.pad(win, ((0, 0), (WINDOW, 0), (0, 0), (0, 0), (0, 0)))

    def one(j):
        st = j * WIN_QBLK
        kw = lax.dynamic_slice_in_dim(win_pad, st, WINDOW + WIN_QBLK, 1)
        return window_attention(lax.dynamic_slice_in_dim(q, st, WIN_QBLK, 1), kw[:, :, 0], kw[:, :, 1],
                                st + jnp.arange(WIN_QBLK), st - WINDOW + jnp.arange(WINDOW + WIN_QBLK))
    o_win = blocked_over_queries(one, T, WIN_QBLK)
    o_nsa = nsa_combine(o_cmp, o_slc, o_win, ngates, ngate)
    y = post_norm(x, o_hg, o_nsa, w_out, ln_g, ln_b)
    return y, rows, win[:, T - min(WINDOW, T):], S.astype(x.dtype)

def sample_layer(x, cache_kv, cache_win, state, page_table, w_in, lb, hg_norm_g,
                 cmp_w1, cmp_w2, cmp_pe, w_out, ln_g, ln_b):
    B, T, _ = x.shape
    hq, hf, hi, hgate, nq, kv, ngates, ngate = split_proj(x, w_in)
    o_hg, S = hgrn2_mix(hq, hf, hi, hgate, state, lb, hg_norm_g)
    q = nq.reshape(B, T, NSA_KV_HEADS, NSA_GROUP, NSA_DH)
    kv = kv.reshape(B, T, 6, NSA_KV_HEADS, NSA_DH).astype(cache_kv.dtype)
    rows_new, win_new = kv[:, :, :4], kv[:, :, 4:]
    past_len = page_table.shape[1] * PAGE_SIZE
    past = cache_kv[page_table].reshape(B, past_len, 4, NSA_KV_HEADS, NSA_DH)
    rows_full = jnp.concatenate([past, rows_new], axis=1)
    qpos = past_len + jnp.arange(T)
    o_cmp, o_slc = nsa_cmp_slc(q, rows_full, qpos, cmp_w1, cmp_w2, cmp_pe, False)
    n_buf = cache_win.shape[1]
    win_cat = jnp.concatenate([cache_win, win_new.astype(cache_win.dtype)], axis=1)
    kpos = past_len - n_buf + jnp.arange(n_buf + T)
    o_win = window_attention(q, win_cat[:, :, 0], win_cat[:, :, 1], qpos, kpos)
    o_nsa = nsa_combine(o_cmp, o_slc, o_win, ngates, ngate)
    y = post_norm(x, o_hg, o_nsa, w_out, ln_g, ln_b)
    return y, rows_new, win_cat[:, T:], S.astype(state.dtype)

def setup_inputs(seed: int = 0) -> dict:
    key = jax.random.key(seed)
    ks = jax.random.split(key, 16)
    nrm = jax.random.normal
    f32 = jnp.float32
    n_pages = PAST_LEN // PAGE_SIZE
    n_pool = (DEC_BATCH * n_pages * 5) // 4
    win_buf = min(WINDOW, PAST_LEN)
    x_prompt = nrm(ks[0], (BATCH, SEQ, D_MODEL), f32)
    x_sample = nrm(ks[1], (DEC_BATCH, DEC_SEQ, D_MODEL), f32)
    cache_kv = nrm(ks[2], (DEPTH, n_pool, PAGE_SIZE, 4, NSA_KV_HEADS, NSA_DH), f32)
    cache_win = nrm(ks[3], (DEPTH, DEC_BATCH, win_buf, 2, NSA_KV_HEADS, NSA_DH), f32)
    state_hgrn = 0.5 * nrm(ks[4], (DEPTH, DEC_BATCH, HG_HEADS, HG_DK, HG_DV), f32)
    page_table = jax.random.permutation(ks[5], n_pool)[:DEC_BATCH * n_pages].reshape(DEC_BATCH, n_pages).astype(jnp.int32)
    w_in = nrm(ks[6], (DEPTH, D_MODEL, D_IN), f32) * D_MODEL ** -0.5
    hg_lb = nrm(ks[7], (DEPTH + 1, D_HG), f32)
    hg_norm_g = 1.0 + 0.02 * nrm(ks[8], (DEPTH, D_HG), f32)
    cmp_w1 = nrm(ks[9], (DEPTH, 2, CMP_L, NSA_DH, CMP_HID), f32) * (CMP_L * NSA_DH) ** -0.5
    cmp_w2 = nrm(ks[10], (DEPTH, 2, CMP_HID, NSA_DH), f32) * CMP_HID ** -0.5
    cmp_pe = 0.5 * nrm(ks[11], (DEPTH, 2, CMP_L, NSA_DH), f32)
    w_out = nrm(ks[12], (DEPTH, D_MODEL, D_MODEL), f32) * (BETA * D_MODEL ** -0.5)
    ln_g = 1.0 + 0.02 * nrm(ks[13], (DEPTH, D_MODEL), f32)
    ln_b = 0.02 * nrm(ks[14], (DEPTH, D_MODEL), f32)
    return {'x_prompt': x_prompt, 'x_sample': x_sample, 'cache_kv': cache_kv, 'cache_win': cache_win,
            'state_hgrn': state_hgrn, 'page_table': page_table, 'w_in': w_in, 'hg_lb': hg_lb,
            'hg_norm_g': hg_norm_g, 'cmp_w1': cmp_w1, 'cmp_w2': cmp_w2, 'cmp_pe': cmp_pe,
            'w_out': w_out, 'ln_g': ln_g, 'ln_b': ln_b}

def reference(x_prompt, x_sample, cache_kv, cache_win, state_hgrn, page_table, w_in, hg_lb,
              hg_norm_g, cmp_w1, cmp_w2, cmp_pe, w_out, ln_g, ln_b):
    lbs = jnp.cumsum(jax.nn.softmax(hg_lb.astype(jnp.float32), axis=0), axis=0)
    yp, ys = x_prompt, x_sample
    kvp, winp, hgp, kvs, wins, hgs = [], [], [], [], [], []
    for layer in range(DEPTH):
        yp, a, b, c = prompt_layer(yp, w_in[layer], lbs[layer], hg_norm_g[layer], cmp_w1[layer],
                                   cmp_w2[layer], cmp_pe[layer], w_out[layer], ln_g[layer], ln_b[layer])
        kvp.append(a)
        winp.append(b)
        hgp.append(c)
        ys, a, b, c = sample_layer(ys, cache_kv[layer], cache_win[layer], state_hgrn[layer], page_table,
                                   w_in[layer], lbs[layer], hg_norm_g[layer], cmp_w1[layer], cmp_w2[layer],
                                   cmp_pe[layer], w_out[layer], ln_g[layer], ln_b[layer])
        kvs.append(a)
        wins.append(b)
        hgs.append(c)
    kv_prompt = jnp.stack(kvp)
    win_prompt = jnp.stack(winp)
    hgrn_prompt = jnp.stack(hgp)
    kv_sample = jnp.stack(kvs)
    win_sample = jnp.stack(wins)
    hgrn_sample = jnp.stack(hgs)
    return (yp, ys, kv_prompt, win_prompt, hgrn_prompt, kv_sample, win_sample, hgrn_sample)


_drawn_inputs = setup_inputs


def setup_inputs(seed=0):
    import zlib

    import numpy as np

    out = dict(_drawn_inputs(seed))
    spreads = {}
    factors = {'cache_kv': 7.487, 'hg_norm_g': 8.0, 'ln_g': 2.755, 'ln_b': 2.788}
    for name, (base, spread) in spreads.items():
        noise = np.random.default_rng([zlib.crc32(name.encode()), seed]).standard_normal(out[name].shape)
        drawn = base * np.exp(spread * noise) if base else spread * noise
        out[name] = jnp.asarray(drawn.astype(out[name].dtype))
    for name, factor in factors.items():
        out[name] = (out[name] * factor).astype(out[name].dtype)
    return out
```

```python
from contextlib import ExitStack

import numpy as np

import concourse.bass as bass
from concourse import mybir

F32 = mybir.dt.float32
I32 = mybir.dt.int32
U32 = mybir.dt.uint32
ALU = mybir.AluOpType
ACT = mybir.ActivationFunctionType
AX_X = mybir.AxisListType.X

P = 128
D = 2048
KT = D // P
SEQ = 512
NB = 8
T = SEQ + NB
TH = T // 2
NQT = SEQ // P
HG = 8
KVH, G, DH = 4, 4, 64
CL, CD = 32, 16
SL = 64
NSEL = 16
PAST, PAGE, NPAGE = 4096, 128, 32
NSUB = PAST // CD
NCMP = NSUB - 1
PSUB = SEQ // CD
PCMP = PSUB - 1
NBLK = PAST // SL
WIN = 512
LEVELS = (64, 32, 16, 8, 4, 2, 1)
NLEV = len(LEVELS) + 1
SCALE = DH ** -0.5
ALPHA = 2.0 ** 0.25
LN_EPS, RMS_EPS = 1e-5, 1e-6
FORCED = 1e4
NEG = -1e30
NQ, NKV, NG = 8, 12, 8
NSTRIP = NQ + NKV + NG + 1
KV0, NG0, BG0 = NQ, NQ + NKV, NQ + NKV + NG
NW = 3 * KVH * G

C_ID, C_ONE, C_CAUS = 0, 128, 256
C_SLOT = 384
C_EXP = C_SLOT + NBLK
C_HALF = C_EXP + 32
C_ROW = C_HALF + 256
C_GRP = C_ROW + 64
C_BD = C_GRP + 4
C_OWN = C_BD + 8
C_EPS = C_OWN + 256
C_N = C_EPS + 2
L_LEV, L_RST = 0, NLEV * 128
L_CM = L_RST + SEQ
L_N = L_CM + NQT * 32


def _constants():
    c = np.zeros((P, C_N), np.float32)
    r = np.arange(P)
    c[:, C_ID:C_ID + P] = np.eye(P)
    c[:, C_ONE:C_ONE + P] = 1.0
    c[:, C_CAUS:C_CAUS + P] = np.where(r[None, :] <= r[:, None], 0.0, NEG)
    c[:, C_SLOT:C_SLOT + NBLK] = np.arange(NBLK)
    for h in range(KVH):
        c[h, C_EXP + 8 * h:C_EXP + 8 * h + 8] = 16.0
        c[4 * h:4 * h + 4, C_GRP + h] = 1.0
        c[4 * h:4 * h + 4, C_OWN + DH * h:C_OWN + DH * h + DH] = 1.0
        for kind in range(2):
            a = C_ROW + (kind * KVH + h) * 8
            c[:, a:a + 8] = (16 * (r % SL) + 4 * (2 + kind) + h)[:, None]
    c[:, C_HALF:C_HALF + P] = (r < SL)
    c[:, C_HALF + P:C_HALF + 2 * P] = (r >= SL)
    c[:NB, C_BD:C_BD + NB] = np.eye(NB)
    c[:, C_EPS] = RMS_EPS
    c[:, C_EPS + 1] = LN_EPS
    return c


def _prompt_constants():
    c = np.zeros((P, L_N), np.float32)
    r = np.arange(P)
    for n, L in enumerate(LEVELS):
        s, t = r[:, None], r[None, :]
        c[:, L_LEV + n * P:L_LEV + (n + 1) * P] = (
            (s // (2 * L) == t // (2 * L)) & (s % (2 * L) < L) & (t % (2 * L) >= L))
    c[:, L_LEV + 7 * P:L_LEV + 8 * P] = np.eye(P)
    c[:, L_RST:L_RST + SEQ] = (np.arange(SEQ) % P != 0)
    for q in range(NQT):
        c[:, L_CM + 32 * q:L_CM + 32 * q + PCMP] = (
            np.arange(PCMP)[None, :] * CD + CL - 1 <= q * P + r[:, None])
    return c


def _semaphores(nc, ctx, prefix=""):
    made = []

    def release():
        nc.clear_and_free_semaphores(made)
        nc.all_engine_barrier()

    def sem(name):
        made.append(nc.alloc_semaphore(prefix + name))
        return made[-1]

    ctx.callback(release)
    return sem


class Leads:

    def __init__(self, *sems):
        self.sems = sems

    def give(self, eng):
        for s in self.sems:
            eng.sem_inc(s, 1)

    def after(self, eng, s, n):
        eng.wait_ge(s, n + any(s is x for x in self.sems))


def hgrn_phase(nc, io, keep):
    const, masks, oT = keep["const"], keep["masks"], keep["oT"]
    cst = lambda a, n: const[:, a:a + n]
    ident, ones = cst(C_ID, P), cst(C_ONE, P)
    with ExitStack() as ctx:
        sb = lambda name, shape, dt=F32: ctx.enter_context(nc.sbuf_tensor(name, shape, dt))
        ps = lambda name, shape: ctx.enter_context(nc.psum_tensor(name, shape, F32))
        sem = _semaphores(nc, ctx)
        xT, w = keep["xT"], keep["w"]
        raw = [sb(n, [P, T]) for n in ("hfT", "hiT", "hqT", "hgT")]
        hf, hi, hq, hg = raw
        lbin = sb("lbin", [P, 2, HG])
        lbx = sb("lbx", [P, 5, HG])
        normg = sb("normg", [P, HG])
        hp = sb("hp", [P, 4])
        en, ep = sb("en", [P, T]), sb("ep", [P, T])
        fT, kT = sb("fT", [P, T]), sb("kT", [P, T])
        logf, A = sb("logf", [P, SEQ]), sb("A", [P, SEQ])
        EA, kd = sb("EA", [P, SEQ]), sb("kd", [P, SEQ])
        qA = sb("qA", [P, SEQ])
        X = [sb(f"X{L}", [P, SEQ]) for L in LEVELS]
        Vn, kdn = sb("Vn", [P, NQT, P]), sb("kdn", [P, NQT, P])
        M, AT = sb("M", [P, NLEV, P]), sb("AT", [P, NQT, P])
        St = sb("St", [P, NQT, P])
        Sold, Snew = sb("Sold", [P, NB, P]), sb("Snew", [P, NB, P])
        kvn = sb("kvn", [NB, 2, P])
        Vbd = sb("Vbd", [NB, NB, P])
        osb, sq, rs, gg = sb("osb", [P, T]), sb("sq", [P, T]), sb("rs", [P, T]), sb("gg", [P, T])
        pj = [ps(f"pj{n}", [P, 2, 512]) for n in range(2)]
        lev = ps("lev", [P, NLEV, P])
        pO = ps("pO", [P, 512])
        pM = ps("pM", [P, NQT, P])

        x_in, par_in = sem("x_in"), sem("par_in")
        w_in = [sem("w_in0"), sem("w_in1")]
        proj, evac = sem("proj"), sem("evac")
        lb_m, lb_s, lb_e, lb_r = sem("lb_m"), sem("lb_s"), sem("lb_e"), sem("lb_r")
        hp_ready = sem("hp_ready")
        exps, fk, fk1, lf, scan = sem("exps"), sem("fk"), sem("fk1"), sem("lf"), sem("scan")
        dlev, elev, xlev = sem("dlev"), sem("elev"), sem("xlev")
        dlast, elast, kd_r, qa_r = sem("dlast"), sem("elast"), sem("kd_r"), sem("qa_r")
        v_t, v_e, s_t, s_e = sem("v_t"), sem("v_e"), sem("s_t"), sem("s_e")
        vbd, outer, sf, snew = sem("vbd"), sem("outer"), sem("sf"), sem("snew")
        kd_t, kd_e, ds = sem("kd_t"), sem("kd_e"), sem("ds")
        lv, mk, at, st = sem("lv"), sem("mk"), sem("at"), sem("st")
        gs, o_c = sem("gs"), sem("o_c")
        o_p, o_e, sqs, ms, lnm, rs_r = sem("o_p"), sem("o_e"), sem("sqs"), sem("ms"), sem("lnm"), sem("rs_r")
        eg, g1, g2, gg_r, nr, fin = sem("eg"), sem("g1"), sem("g2"), sem("gg_r"), sem("nr"), sem("fin")
        old_in, st_out, new_out = sem("old_in"), sem("st_out"), sem("new_out")
        leads = Leads(st, o_e, lnm, fk, fin, at, st_out, new_out)
        after = leads.after
        block = ctx.enter_context(nc.Block())

        @block.gpsimd
        def _(pool):
            leads.give(pool)

        @block.sync
        def _(sp):
            sp.dma_start(lbin[:], io["hg_lb"]).then_inc(par_in, 16)
            sp.dma_start(normg[:], io["norm_g"]).then_inc(par_in, 16)
            sp.dma_start(const[:], io["const"]).then_inc(par_in, 16)
            sp.dma_start(masks[:], io["masks"]).then_inc(par_in, 16)
            sp.dma_start(w[0], io["w_in"][0]).then_inc(w_in[0], 16)
            for a in range(4):
                sp.dma_start(xT[:, 4 * a:4 * a + 4], io["xT"][:, 4 * a:4 * a + 4]).then_inc(x_in, 16)
            sp.dma_start(w[1], io["w_in"][1]).then_inc(w_in[1], 16)

            def load(h, js):
                for j in js:
                    after(sp, proj, 4 * h + j - 1)
                    sp.dma_start(w[j % 2], io["w_in"][bass.ds(4 * h + j, 1)]
                                 .rearrange("a p k e -> p (a k) e")).then_inc(w_in[j % 2], 16)

            def states(h, last):
                after(sp, st, 4 * h + 4)
                sp.dma_start(io["hgrn_prompt"][bass.ds(h, 1)].rearrange("a k v -> k (a v)"),
                             St[:, 3, :]).then_inc(st_out, 16)
                after(sp, snew, h + 1)
                sp.dma_start(io["hgrn_sample"][:, bass.ds(h, 1)].rearrange("b a k v -> k (b a) v"),
                             Snew[:]).then_inc(new_out, 16)
                if not last:
                    load_state(h + 1)

            def load_state(h):
                sp.dma_start(Sold[:], io["state"][:, bass.ds(h, 1)]
                             .rearrange("b a k v -> k (b a) v")).then_inc(old_in, 16)

            load(0, (2, 3))
            load_state(0)
            with sp.Fori(0, HG - 1) as i:
                load(i + 1, (0, 1))
                states(i, False)
                load(i + 1, (2, 3))
            states(HG - 1, True)
            after(sp, st_out, 16 * HG)
            after(sp, new_out, 16 * HG)

        @block.tensor
        def _(pe):
            def project(h, j, part):
                b = j % 2
                if part == 0:
                    after(pe, w_in[b], 32 * h + 16 * (j // 2 + 1))
                    if not (isinstance(h, int) and 4 * h + j < 2):
                        after(pe, evac, 4 * h + j - 1)
                for k in range(8 * part, 8 * part + 8):
                    for a in range(2):
                        mm = nc.tensor.matmul(pj[b][:, a, 0:TH], w[b][:, k, :], xT[:, k, a * TH:(a + 1) * TH],
                                              start=(k == 0), stop=(k == KT - 1))
                if part == 1:
                    mm.then_inc(proj, 1)

            def turn_values(h):
                after(pe, evac, 4 * h + 2)
                after(pe, st, 4 * h)
                after(pe, o_e, h)
                for c in range(NQT):
                    mm = nc.tensor.transpose(pM[:, c, :], hi[:, c * P:(c + 1) * P], ident)
                mm.then_inc(v_t, 1)
                after(pe, fk, h + 1)
                nc.tensor.transpose(pO[0:NB, 0:P], kT[:, SEQ:T], ident)
                nc.tensor.transpose(pO[0:NB, P:2 * P], hi[:, SEQ:T], ident).then_inc(s_t, 1)

            def turn_decayed(h):
                after(pe, kd_r, h + 1)
                after(pe, v_e, h + 1)
                for c in range(NQT):
                    mm = nc.tensor.transpose(pM[:, c, :], kd[:, c * P:(c + 1) * P], ident)
                mm.then_inc(kd_t, 1)
                after(pe, vbd, h + 1)
                after(pe, lnm, 2 * h)
                for a in range(2):
                    mm = nc.tensor.matmul(lev[:, 4 * a:4 * a + 4, :], kvn[:, 0, :], Vbd[:, 4 * a:4 * a + 4, :],
                                          start=True, stop=True)
                mm.then_inc(outer, 1)

            def state_terms(h):
                after(pe, kd_e, h + 1)
                for c in range(NQT):
                    mm = nc.tensor.matmul(pM[:, c, :], kdn[:, c, :], Vn[:, c, :], start=True, stop=True)
                mm.then_inc(ds, 1)

            def levels(h, c):
                if c == 0:
                    after(pe, xlev, 7 * h + 7)
                    after(pe, snew, h + 1)
                    after(pe, evac, 4 * h + 3)
                else:
                    after(pe, mk, 4 * h + c)
                cols = slice(c * P, (c + 1) * P)
                for n in range(NLEV):
                    left, right = (X[n], X[n]) if n < 7 else (kT, hq)
                    mm = nc.tensor.matmul(lev[:, n, :], left[:, cols], right[:, cols], start=True, stop=True)
                mm.then_inc(lv, 1)

            def outputs(h):
                after(pe, s_e, h + 1)
                for c in range(NQT):
                    cols = slice(c * P, (c + 1) * P)
                    after(pe, at, 4 * h + c + 1)
                    nc.tensor.matmul(pO[:, cols], Vn[:, c, :], AT[:, c, :], start=True, stop=(c == 0))
                    if c:
                        after(pe, st, 4 * h + c)
                        after(pe, qa_r, h + 1)
                        nc.tensor.matmul(pO[:, cols], St[:, c - 1, :], qA[:, cols], start=False, stop=True)
                after(pe, st, 4 * h + 4)
                after(pe, snew, h + 1)
                for b in range(NB):
                    mm = nc.tensor.matmul(pM[:, 0, b:b + 1], Snew[:, b, :], hq[:, SEQ + b:SEQ + b + 1],
                                          start=True, stop=True)
                mm.then_inc(o_p, 1)

            def mean_squares(h):
                after(pe, sqs, h + 1)
                after(pe, mk, 4 * h + 4)
                nc.tensor.matmul(lev[:, 0:4, :], ones, sq[:, 0:SEQ], start=True, stop=True)
                nc.tensor.matmul(lev[:, 4, 0:NB], ones, sq[:, SEQ:T], start=True, stop=True).then_inc(ms, 1)

            after(pe, par_in, 64)
            after(pe, x_in, 64)
            for j in range(4):
                project(0, j, 0)
                project(0, j, 1)
            with pe.Fori(0, HG - 1) as i:
                project(i + 1, 0, 0)
                project(i + 1, 0, 1)
                turn_values(i)
                project(i + 1, 1, 0)
                turn_decayed(i)
                project(i + 1, 1, 1)
                state_terms(i)
                levels(i, 0)
                project(i + 1, 2, 0)
                levels(i, 1)
                levels(i, 2)
                project(i + 1, 2, 1)
                levels(i, 3)
                project(i + 1, 3, 0)
                outputs(i)
                project(i + 1, 3, 1)
                mean_squares(i)
            h = HG - 1
            turn_values(h)
            turn_decayed(h)
            state_terms(h)
            for c in range(NQT):
                levels(h, c)
            outputs(h)
            mean_squares(h)

        @block.scalar
        def _(act):
            def empty(h, j, free=None):
                after(act, proj, 4 * h + j + 1)
                if free:
                    after(act, *free)
                nc.scalar.activation(raw[j][:].rearrange("p (a t) -> p a t", a=2), pj[j % 2][:, :, 0:TH],
                                     ACT.Copy).then_inc(evac, 1)

            def first(h):
                after(act, evac, 4 * h + 1)
                after(act, fk, h)
                nc.scalar.activation(en[:], hf[:], ACT.Sigmoid)
                nc.scalar.activation(ep[:], hf[:], ACT.Sigmoid, scale=-1.0).then_inc(exps, 1)
                after(act, evac, 4 * h + 4)
                after(act, fin, h)
                nc.scalar.activation(gg[:], hg[:], ACT.Sigmoid).then_inc(eg, 1)
                after(act, fk1, h + 1)
                nc.scalar.activation(logf[:], fT[:, 0:SEQ], ACT.Ln).then_inc(lf, 1)
                after(act, dlast, h + 1)
                nc.scalar.activation(EA[:], A[:], ACT.Exp)
                nc.scalar.activation(kd[:], kd[:], ACT.Exp).then_inc(elast, 1)
                for n in range(7):
                    after(act, dlev, 7 * h + n + 1)
                    nc.scalar.activation(X[n][:], X[n][:], ACT.Exp).then_inc(elev, 1)

            def values(h):
                after(act, v_t, h + 1)
                nc.scalar.activation(Vn[:], pM[:], ACT.Copy).then_inc(v_e, 1)

            def decayed(h):
                after(act, kd_t, h + 1)
                nc.scalar.activation(kdn[:], pM[:], ACT.Copy).then_inc(kd_e, 1)

            def norm(h):
                after(act, ms, h + 1)
                nc.scalar.activation(rs[:, 0:SEQ].rearrange("p (a b) -> p a b", a=4), lev[:, 0:4, :], ACT.Ln,
                                     scale=1.0 / P, bias=const[:, C_EPS:C_EPS + 1]).then_inc(lnm, 1)
                nc.scalar.activation(rs[:, SEQ:T], lev[:, 4, 0:NB], ACT.Ln,
                                     scale=1.0 / P, bias=const[:, C_EPS:C_EPS + 1]).then_inc(lnm, 1)
                after(act, lnm, 2 * h + 2)
                nc.scalar.activation(rs[:], rs[:], ACT.Exp, scale=-0.5).then_inc(rs_r, 1)

            after(act, lb_s, 1)
            nc.scalar.activation(lbx[:, 1:3, :], lbx[:, 1:3, :], ACT.Exp).then_inc(lb_e, 1)
            for j in range(4):
                empty(0, j)
            with act.Fori(0, HG - 1) as i:
                first(i)
                empty(i + 1, 0)
                values(i)
                decayed(i)
                empty(i + 1, 1, (s_t, i + 1))
                empty(i + 1, 2, (o_p, i + 1))
                norm(i)
                empty(i + 1, 3, (gg_r, i + 1))
            h = HG - 1
            first(h)
            values(h)
            decayed(h)
            norm(h)

        @block.vector
        def _(v):
            def halves(t, L):
                return t.rearrange("p (n a l) -> p n a l", a=2, l=L)

            def spread(t, n, m):
                return t.unsqueeze(2).to_broadcast([P, n, m])

            after(v, par_in, 64)
            nc.vector.tensor_tensor(lbx[:, 0, :], lbin[:, 0, :], lbin[:, 1, :], ALU.max).then_inc(lb_m, 1)
            after(v, lb_m, 1)
            nc.vector.tensor_tensor(lbx[:, 1:3, :], lbin[:], lbx[:, 0:1, :].to_broadcast([P, 2, HG]),
                                    ALU.subtract).then_inc(lb_s, 1)
            after(v, lb_e, 1)
            nc.vector.tensor_tensor(lbx[:, 0, :], lbx[:, 1, :], lbx[:, 2, :], ALU.add).then_inc(lb_r, 1)
            after(v, lb_r, 1)
            nc.vector.reciprocal(lbx[:, 0, :], lbx[:, 0, :]).then_inc(lb_r, 1)
            after(v, lb_r, 2)
            nc.vector.tensor_tensor(lbx[:, 3, :], lbx[:, 1, :], lbx[:, 0, :], ALU.mult).then_inc(lb_r, 1)
            nc.vector.tensor_tensor(lbx[:, 4, :], lbx[:, 2, :], lbx[:, 0, :], ALU.mult).then_inc(lb_r, 1)
            after(v, lb_r, 4)

            def gates(h):
                nc.vector.tensor_copy(hp[:, 0:2].unsqueeze(2), lbx[:, 3:5, bass.ds(h, 1)])
                nc.vector.tensor_copy(hp[:, 2:3], normg[:, bass.ds(h, 1)]).then_inc(hp_ready, 1)
                after(v, exps, h + 1)
                after(v, hp_ready, h + 1)
                nc.vector.tensor_scalar(fT[:], en[:], hp[:, 1:2], hp[:, 0:1], ALU.mult, ALU.add).then_inc(fk1, 1)
                nc.vector.tensor_scalar(kT[:], ep[:], hp[:, 1:2], None, ALU.mult).then_inc(fk, 1)
                after(v, lf, h + 1)
                nc.vector.tensor_tensor_scan(A[:], masks[:, L_RST:L_RST + SEQ], logf[:], 0.0,
                                             ALU.mult, ALU.add).then_inc(scan, 1)
                after(v, scan, h + 1)
                A4, kd4 = (t[:].rearrange("p (c t) -> p c t", c=NQT) for t in (A, kd))
                nc.vector.tensor_tensor(kd4, A4[:, :, P - 1:P].to_broadcast([P, NQT, P]), A4,
                                        ALU.subtract).then_inc(dlast, 1)
                for n, L in enumerate(LEVELS):
                    a, x = halves(A[:], L), halves(X[n][:], L)
                    mid = a[:, :, 0, L - 1:L].to_broadcast([P, SEQ // (2 * L), L])
                    nc.vector.tensor_tensor(x[:, :, 0, :], mid, a[:, :, 0, :], ALU.subtract)
                    nc.vector.tensor_tensor(x[:, :, 1, :], a[:, :, 1, :], mid, ALU.subtract).then_inc(dlev, 1)

            def decays(h):
                after(v, elast, h + 1)
                after(v, fk, h + 1)
                nc.vector.tensor_tensor(kd[:], kd[:], kT[:, 0:SEQ], ALU.mult).then_inc(kd_r, 1)
                after(v, evac, 4 * h + 3)
                nc.vector.tensor_tensor(qA[:], EA[:], hq[:, 0:SEQ], ALU.mult).then_inc(qa_r, 1)
                for n, L in enumerate(LEVELS):
                    after(v, elev, 7 * h + n + 1)
                    x = halves(X[n][:], L)
                    nc.vector.tensor_tensor(x[:, :, 0, :], x[:, :, 0, :], halves(kT[:, 0:SEQ], L)[:, :, 0, :],
                                            ALU.mult)
                    nc.vector.tensor_tensor(x[:, :, 1, :], x[:, :, 1, :], halves(hq[:, 0:SEQ], L)[:, :, 1, :],
                                            ALU.mult).then_inc(xlev, 1)

            def decode_states(h):
                after(v, s_t, h + 1)
                nc.vector.tensor_copy(kvn[:], pO[0:NB, 0:2 * P].rearrange("p (a b) -> p a b", a=2)).then_inc(s_e, 1)
                after(v, s_e, h + 1)
                nc.vector.tensor_tensor(Vbd[:], kvn[:, 1:2, :].to_broadcast([NB, NB, P]),
                                        const[0:NB, C_BD:C_BD + NB].unsqueeze(2).to_broadcast([NB, NB, P]),
                                        ALU.mult).then_inc(vbd, 1)
                after(v, old_in, 16 * h + 16)
                after(v, new_out, 16 * h)
                nc.vector.tensor_tensor(Snew[:], Sold[:], spread(fT[:, SEQ:T], NB, P), ALU.mult).then_inc(sf, 1)
                after(v, sf, h + 1)
                after(v, outer, h + 1)
                nc.vector.tensor_tensor(Snew[:], Snew[:], lev[:], ALU.add).then_inc(snew, 1)

            def prompt_states(h):
                after(v, ds, h + 1)
                after(v, st_out, 16 * h)
                nc.vector.tensor_copy(St[:, 0, :], pM[:, 0, :]).then_inc(st, 1)
                for c in range(1, NQT):
                    after(v, st, 4 * h + c)
                    nc.vector.scalar_tensor_tensor(St[:, c, :], St[:, c - 1, :], EA[:, c * P + P - 1:c * P + P],
                                                   pM[:, c, :], ALU.mult, ALU.add).then_inc(st, 1)

            def level(h, c):
                after(v, lv, 4 * h + c + 1)
                after(v, at, 4 * h + c)
                nc.vector.tensor_tensor(M[:].rearrange("p n t -> p (n t)"), lev[:].rearrange("p n t -> p (n t)"),
                                        masks[:, L_LEV:L_LEV + NLEV * P], ALU.mult).then_inc(mk, 1)
                after(v, mk, 4 * h + c + 1)
                nc.vector.tensor_reduce(AT[:, c, :], M[:].rearrange("p n t -> p t n"), AX_X,
                                        ALU.add).then_inc(at, 1)

            def finish(h):
                after(v, eg, h + 1)
                nc.vector.tensor_tensor(gg[:], gg[:], hg[:], ALU.mult).then_inc(gg_r, 1)
                after(v, o_p, h + 1)
                nc.vector.tensor_copy(osb[:, 0:SEQ], pO[:]).then_inc(o_c, 1)
                nc.vector.tensor_copy(osb[:, SEQ:T], pM[:, 0, 0:NB]).then_inc(o_e, 1)
                after(v, o_c, h + 1)
                after(v, o_e, h + 1)
                nc.vector.tensor_tensor(sq[:], osb[:], osb[:], ALU.mult).then_inc(sqs, 1)
                after(v, rs_r, h + 1)
                nc.vector.scalar_tensor_tensor(osb[:], osb[:], hp[:, 2:3], rs[:], ALU.mult, ALU.mult).then_inc(nr, 1)
                after(v, nr, h + 1)
                after(v, gg_r, h + 1)
                nc.vector.tensor_tensor(oT[:, bass.ds(h, 1), :].rearrange("p a t -> p (a t)"), osb[:], gg[:],
                                        ALU.mult).then_inc(fin, 1)

            with v.Fori(0, HG) as h:
                gates(h)
                decays(h)
                decode_states(h)
                prompt_states(h)
                for c in range(NQT):
                    level(h, c)
                finish(h)


def projection_phase(nc, io, keep):
    xT, w, hN = keep["xT"], keep["w"], keep["hN"]
    with ExitStack() as ctx:
        sem = _semaphores(nc, ctx)
        pj = [ctx.enter_context(nc.psum_tensor(f"pn{n}", [P, 2, 512], F32)) for n in range(2)]
        w_in = [sem("nw_in0"), sem("nw_in1")]
        proj = sem("n_proj")
        evac = [sem("n_evac0"), sem("n_evac1")]
        leads = Leads(*evac)
        after = leads.after
        pairs = NSTRIP // 2
        block = ctx.enter_context(nc.Block())

        @block.gpsimd
        def _(pool):
            leads.give(pool)

        def filled(n, i):
            return (hN[:, bass.ds(2 * i + n, 1), :].rearrange("p s (a t) -> p (s a) t", a=2), pj[n][:, :, 0:TH])

        @block.sync
        def _(sp):
            def load(n, i):
                sp.dma_start(w[n], io["w_in"][bass.ds(4 * HG + 2 * i + n, 1)]
                             .rearrange("a p k e -> p (a k) e")).then_inc(w_in[n], 16)
            load(0, 0)
            load(1, 0)
            with sp.Fori(1, pairs) as i:
                for n in range(2):
                    after(sp, proj, 2 * i + n - 1)
                    load(n, i)
            after(sp, proj, 2 * pairs - 1)
            load(0, pairs)

        @block.tensor
        def _(pe):
            def project(n, i):
                after(pe, w_in[n], 16 * i + 16)
                after(pe, evac[n], i)
                for k in range(KT):
                    for a in range(2):
                        mm = nc.tensor.matmul(pj[n][:, a, 0:TH], w[n][:, k, :], xT[:, k, a * TH:(a + 1) * TH],
                                              start=(k == 0), stop=(k == KT - 1))
                mm.then_inc(proj, 1)
            with pe.Fori(0, pairs) as i:
                project(0, i)
                project(1, i)
            project(0, pairs)

        @block.scalar
        def _(act):
            with act.Fori(0, pairs + 1) as i:
                after(act, proj, 2 * i + 1)
                nc.scalar.activation(*filled(0, i), ACT.Copy).then_inc(evac[0], 1)

        @block.vector
        def _(v):
            with v.Fori(0, pairs) as i:
                after(v, proj, 2 * i + 2)
                nc.vector.tensor_copy(*filled(1, i)).then_inc(evac[1], 1)


class Chain:

    def __init__(self, eng, sem, i, n, plain=None):
        self.eng, self.sem, self.start, self.n, self.k, self.plain = eng, sem, i * n, n, 0, plain

    def __call__(self, instruction, before_plain=False):
        instruction.then_inc(self.sem, 1)
        self.k += 1
        self.eng.wait_ge(self.sem, self.start + self.k)
        if before_plain:
            self.plain(self.eng)

    def end(self):
        assert self.k == self.n, self.k


def rows_phase(nc, io, keep):
    const, hN, NV, gN, gS = (keep[n] for n in ("const", "hN", "NV", "gN", "gS"))
    w1, w2p, w2v, hb = keep["w1"], keep["w2p"], keep["w2v"], keep["hb"]
    kcT, vc = keep["kcT_p"], keep["vc_p"]
    ident = const[:, C_ID:C_ID + P]
    with ExitStack() as ctx:
        sb = lambda name, shape, dt=F32: ctx.enter_context(nc.sbuf_tensor(name, shape, dt))
        ps = lambda name, shape: ctx.enter_context(nc.psum_tensor(name, shape, F32))
        sem = _semaphores(nc, ctx)
        kvn = sb("kv_new", [NB, 6 * KVH * DH])
        pe_in = sb("pe_in", [P, 2, CL // 2])
        XT = keep["xT"][:].rearrange("p k t -> p (k t)")[:, NQT * 1536:NQT * 1536 + 2 * KVH * CD // 2 * PSUB]
        XT = XT.rearrange("p (a h j n) -> p a h j n", a=2, h=KVH, j=CD // 2)
        sg = sb("sg_p", [P, 2, KVH, PCMP])
        hs = sb("hs_p", [P, 2, KVH, PCMP])
        gx = sb("gx", [P, 2, T])
        tb = [ps(f"tb{n}", [P, 512]) for n in range(2)]
        pB = ps("pB", [P, 512])
        pH = ps("pH", [P, 2, KVH, 32])
        pK = ps("pK", [P, 512])
        par_in, turned, copied, gated = sem("c_par"), sem("turned"), sem("copied"), sem("gated")
        w2z, w2s = sem("w2z"), sem("w2s")
        rows_out, new_out = sem("rows_out"), sem("newr_out")
        bias, bias_r = sem("bias"), sem("bias_r")
        gsig, gmul, bg_t = sem("gsig"), sem("gmul"), sem("bg_t")
        xc, hid, hsig, hs_r, kct, kv_r = (sem(n) for n in ("xc", "hid", "hsig", "hs_r", "kct", "kv_r"))
        block = ctx.enter_context(nc.Block())
        groups = [(c, g) for c in range(NQT + 1) for g in range(3)]

        @block.sync
        def _(sp):
            sp.dma_start(pe_in[:], io["pe"]).then_inc(par_in, 16)
            sp.dma_start(w1[:], io["w1"]).then_inc(par_in, 16)
            sp.dma_start(w2v[:], io["w2"]).then_inc(par_in, 16)
            for c in range(NQT):
                sp.wait_ge(copied, 3 * c + 3)
                sp.dma_start(io["kv_prompt"][c * P:(c + 1) * P], NV[:, c, 0:1024]).then_inc(rows_out, 16)
                sp.dma_start(io["win_prompt"][c * P:(c + 1) * P], NV[:, c, 1024:1536]).then_inc(rows_out, 16)
            sp.wait_ge(copied, 3 * NQT + 3)
            sp.dma_start(io["kv_sample"], kvn[:, 0:1024]).then_inc(new_out, 16)
            sp.dma_start(io["new_rows"], kvn[:]).then_inc(new_out, 16)
            sp.wait_ge(rows_out, 32 * NQT)
            sp.wait_ge(new_out, 32)

        @block.tensor
        def _(pe):
            for n, (c, g) in enumerate(groups):
                if n >= 2:
                    pe.wait_ge(copied, n - 1)
                cols, m = (slice(c * P, (c + 1) * P), P) if c < NQT else (slice(SEQ, T), NB)
                for s in range(4):
                    mm = nc.tensor.transpose(tb[n % 2][0:m, s * P:(s + 1) * P], hN[:, KV0 + 4 * g + s, cols], ident)
                mm.then_inc(turned, 1)
            for c in range(NQT):
                mm = nc.tensor.transpose(pK[:, c * P:(c + 1) * P], hN[:, BG0, c * P:(c + 1) * P], ident)
            mm.then_inc(bg_t, 1)
            pe.wait_ge(par_in, 48)
            for kind in range(2):
                for n in range(CL // 2):
                    mm = nc.tensor.matmul(pB[:, kind:kind + 1], w1[:, kind, n, :], pe_in[:, kind, n:n + 1],
                                          start=(n == 0), stop=(n == CL // 2 - 1))
            mm.then_inc(bias, 1)
            pe.wait_ge(xc, 4 * KVH)
            for kind in range(2):
                for n in range(CL // 2):
                    r, jp = divmod(n, CD // 2)
                    mm = nc.tensor.matmul(pH[:, kind, :, 0:PCMP], w1[:, kind, n, :],
                                          XT[:, kind, :, jp, r:r + PCMP],
                                          start=(n == 0), stop=(n == CL // 2 - 1))
            mm.then_inc(hid, 1)
            pe.wait_ge(hs_r, 2)
            pe.wait_ge(w2s, 2)
            pe.wait_ge(gated, 1)
            for hp in range(2):
                for par in range(2):
                    nc.tensor.matmul(pK[:, hp * 32:hp * 32 + PCMP], w2p[:, par, :], hs[:, 0, 2 * hp + par, :],
                                     start=(par == 0), stop=(par == 1))
            for h in range(KVH):
                mm = nc.tensor.matmul(pK[0:PCMP, 64 + h * DH:64 + (h + 1) * DH], hs[:, 1, h, :], w2v[:, 1, :],
                                      start=True, stop=True)
            mm.then_inc(kct, 1)

        @block.scalar
        def _(act):
            act.wait_ge(bg_t, 1)
            nc.scalar.activation(gN[:].rearrange("p c n -> p (c n)"), pK[:], ACT.Sigmoid).then_inc(gated, 1)
            for n in range(3):
                nc.scalar.activation(gS[0:16, n, :], hN[32 * n:32 * n + 16, BG0, SEQ:T], ACT.Sigmoid)
            for n in range(NG // 2):
                if n:
                    act.wait_ge(gmul, n)
                nc.scalar.activation(gx[:], hN[:, NG0 + 2 * n:NG0 + 2 * n + 2, :], ACT.Sigmoid).then_inc(gsig, 1)
            act.wait_ge(hid, 1)
            act.wait_ge(bias_r, 1)
            for kind in range(2):
                nc.scalar.activation(sg[:, kind], pH[:, kind, :, 0:PCMP], ACT.Sigmoid,
                                     bias=hb[:, kind:kind + 1]).then_inc(hsig, 1)

        @block.gpsimd
        def _(pool):
            for n in range(2 * KVH):
                par = n % 2
                rows = (hN[par * DH:(par + 1) * DH, KV0 + n // 2, 0:SEQ]
                        .rearrange("p (n j a) -> p a j n", j=CD // 2, a=2))
                for a in range(2):
                    nc.gpsimd.tensor_copy(XT[a * DH:(a + 1) * DH, n // KVH, n % KVH], rows[:, a]).then_inc(xc, 1)
                    pool.wait_ge(xc, 2 * n + a + 1)
            nc.gpsimd.memset(w2p[:], 0.0).then_inc(w2z, 1)
            pool.wait_ge(w2z, 1)
            pool.wait_ge(par_in, 48)
            for par in range(2):
                nc.gpsimd.tensor_copy(w2p[:, par, par * DH:(par + 1) * DH], w2v[:, 0, :]).then_inc(w2s, 1)

        @block.vector
        def _(v):
            for n, (c, g) in enumerate(groups):
                v.wait_ge(turned, n + 1)
                dst, m = (NV[:, c, :], P) if c < NQT else (kvn[:], NB)
                nc.vector.tensor_copy(dst[:, g * 512:(g + 1) * 512], tb[n % 2][0:m, :]).then_inc(copied, 1)
            v.wait_ge(bias, 1)
            nc.vector.tensor_copy(hb[:], pB[:, 0:2]).then_inc(bias_r, 1)
            for n in range(NG // 2):
                v.wait_ge(gsig, n + 1)
                s = hN[:, NG0 + 2 * n:NG0 + 2 * n + 2, :]
                nc.vector.tensor_tensor(s, s, gx[:], ALU.mult).then_inc(gmul, 1)
            v.wait_ge(bias_r, 1)
            for kind in range(2):
                v.wait_ge(hsig, 2)
                nc.vector.scalar_tensor_tensor(hs[:, kind], pH[:, kind, :, 0:PCMP], hb[:, kind:kind + 1],
                                               sg[:, kind], ALU.add, ALU.mult).then_inc(hs_r, 1)
            v.wait_ge(kct, 1)
            nc.vector.tensor_copy(kcT[:], pK[:, 0:64].rearrange("p (a n) -> p a n", a=2)[:, :, 0:PCMP])
            nc.vector.tensor_copy(vc[0:PCMP, :], pK[0:PCMP, 64:320])
            v.wait_ge(gmul, NG // 2)
            nc.vector.tensor_copy(keep["qS"][:], hN[:, 0:NQ, SEQ:T])
            nc.vector.tensor_copy(keep["ngS"][:], hN[:, NG0:NG0 + NG, SEQ:T]).then_inc(kv_r, 1)


def prompt_phase(nc, io, keep):
    const, hN, NV, gN, oT = (keep[n] for n in ("const", "hN", "NV", "gN", "oT"))
    kcT, vc = keep["kcT_p"], keep["vc_p"]
    ident = const[:, C_ID:C_ID + P]
    NU = 2 * NQT
    with ExitStack() as ctx:
        sb = lambda name, shape, dt=F32: ctx.enter_context(nc.sbuf_tensor(name, shape, dt))
        ps = lambda name, shape: ctx.enter_context(nc.psum_tensor(name, shape, F32))
        sem = _semaphores(nc, ctx)
        Q, Kf, kcf = sb("Q", [P, SEQ]), sb("Kf", [P, 2, SEQ]), sb("kcf", [P, PCMP])
        cs, cneg = sb("cs", [P, 2, NQT, 32]), sb("cneg", [P, NQT, 32])
        cmx, cden, crd = sb("cmx", [P, 2, NQT]), sb("cden", [P, 2, NQT]), sb("crd", [P, 2, NQT])
        mx, nm = [sb(f"mx{n}", [P, 2]) for n in range(2)], [sb(f"nm{n}", [P, 2]) for n in range(2)]
        den, rd = sb("den", [P, NU, 2]), sb("rd", [P, 3])
        flat = [t.rearrange("p k e -> p (k e)") for t in keep["w"]]
        Pb = [t[:, 0:1024].rearrange("p (a n) -> p a n", a=2) for t in flat]
        PT = [t[:, 1024:2048].rearrange("p (a c n) -> p a c n", a=2, c=NQT) for t in flat]
        PTc = sb("PTc", [32, NU, P])
        oN = sb("oN", [P, NQT, 2, DH])
        acc = sb("acc_p", [P, 2, DH])
        pS = [ps(f"pS{n}", [P, 2, 512]) for n in range(2)]
        pT = ps("pT", [P, 2, NQT, P])
        pC = ps("pC", [P, 512])
        pX = ps("pX", [P, NQT, P])
        names = ("q_r k_r c_s c_add c_max c_sub c_exp c_mul c_sum c_top c_rd ct ct_e s_p m_d m_x nm_r p_e pt "
                 "pe_a pe_v pv rd_a rd_b a0 a1 a2 on ot fin2 cn cn1")
        S = {n: sem("p_" + n) for n in names.split()}
        (q_r, k_r, c_s, c_add, c_max, c_sub, c_exp, c_mul, c_sum, c_top, c_rd, ct, ct_e, s_p, m_d, m_x, nm_r, p_e,
         pt, pe_a, pe_v, pv, rd_a, rd_b, a0, a1, a2, on, ot, fin, cn, cn1) = S.values()
        leads = Leads(*S.values())
        after = leads.after
        block = ctx.enter_context(nc.Block())

        def width(u):
            return (u % NQT + 1) * P

        @block.gpsimd
        def _(pool):
            leads.give(pool)
            with pool.Fori(0, 2) as hp:
                after(pool, pv, hp * 4 * NU)
                for n in range(2):
                    nc.gpsimd.tensor_copy(Kf[:, n, :], hN[:, bass.ds(hp + KV0 + 4 * n + 4, 1), 0:SEQ]
                                          .rearrange("p a t -> p (a t)"))
                nc.gpsimd.tensor_copy(kcf[:], kcT[:, bass.ds(hp, 1), :].rearrange("p a t -> p (a t)"))
                with pool.Fori(0, G) as g:
                    i = hp * G + g
                    after(pool, s_p, i * NU)
                    nc.gpsimd.tensor_copy(Q[:], hN[:, bass.ds(i, 1), 0:SEQ].rearrange("p a t -> p (a t)")
                                          ).then_inc(q_r, 1)

        @block.tensor
        def _(pe):
            def scores(i, u):
                par, qt = divmod(u, NQT)
                rows, cols, n = slice(par * DH, (par + 1) * DH), slice(qt * P, (qt + 1) * P), width(u)
                after(pe, p_e, i * NU + max(u - 1, 0))
                for br in range(2):
                    mm = nc.tensor.matmul(pS[u % 2][:, br, 0:n], Q[rows, cols], Kf[rows, br, 0:n],
                                          start=True, stop=True)
                mm.then_inc(s_p, 1)

            def turn(i, u):
                after(pe, p_e, i * NU + u + 1)
                if u:
                    after(pe, pe_a, i * NU + u)
                    after(pe, pe_v, i * NU + u)
                else:
                    after(pe, ct_e, i + 1)
                for br in range(2):
                    for c in range(width(u) // P):
                        mm = nc.tensor.transpose(pT[:, br, c, :], Pb[u % 2][:, br, c * P:(c + 1) * P], ident)
                mm.then_inc(pt, 1)

            def values(i, hp, u):
                par = u // NQT
                after(pe, pe_a, i * NU + u + 1)
                after(pe, pe_v, i * NU + u + 1)
                after(pe, a2, i * NU + u)
                for br, kind in ((0, 3), (1, 5)):
                    k = width(u) // P
                    for c in range(k):
                        nc.tensor.matmul(pC[:, 256 + DH * br:256 + DH * br + DH], PT[u % 2][:, br, c, :],
                                         NV[:, c, bass.ds(hp * P + (kind * 256 + par * DH), DH)],
                                         start=(c == 0), stop=(c == k - 1))
                nc.tensor.matmul(pC[:, 256 + 2 * DH:256 + 3 * DH], PTc[0:PCMP, u, :],
                                 vc[0:PCMP, bass.ds(hp * P + par * DH, DH)],
                                 start=True, stop=True).then_inc(pv, 1)

            def step(hp, g):
                i = hp * G + g
                after(pe, q_r, i + 1)
                after(pe, c_add, i)
                after(pe, a2, i * NU)
                after(pe, fin, i)
                for u in range(NU):
                    par, qt = divmod(u, NQT)
                    rows, cols = slice(par * DH, (par + 1) * DH), slice(qt * P, (qt + 1) * P)
                    bank = pC if par == 0 else pX[:].rearrange("p q n -> p (q n)")
                    mm = nc.tensor.matmul(bank[:, 32 * qt:32 * qt + PCMP], Q[rows, cols], kcf[rows, :],
                                          start=True, stop=True)
                mm.then_inc(c_s, 1)
                scores(i, 0)
                scores(i, 1)
                after(pe, c_mul, i + 1)
                after(pe, pe_a, i * NU)
                after(pe, pe_v, i * NU)
                for u in range(NU):
                    par, qt = divmod(u, NQT)
                    mm = nc.tensor.transpose(pT[0:PCMP, par, qt, :], cs[:, par, qt, 0:PCMP], ident)
                mm.then_inc(ct, 1)
                turn(i, 0)
                for u in range(NU):
                    if u + 2 < NU:
                        scores(i, u + 2)
                    if u + 1 < NU:
                        turn(i, u + 1)
                    values(i, hp, u)
                after(pe, a2, (i + 1) * NU)
                for qt in range(NQT):
                    mm = nc.tensor.transpose(pX[:, qt, :], oN[:, qt].rearrange("p a d -> p (a d)"), ident)
                mm.then_inc(ot, 1)

            with pe.Fori(0, 2) as hp:
                with pe.Fori(0, G) as g:
                    step(hp, g)

        @block.scalar
        def _(act):
            def exps(i, u):
                after(act, nm_r, i * NU + u + 1)
                after(act, rd_a, i * NU)
                after(act, pt, i * NU + u - 1 if u else i * NU)
                n = width(u)
                for br in range(2):
                    ins = nc.scalar.activation(Pb[u % 2][:, br, 0:n], pS[u % 2][:, br, 0:n], ACT.Exp,
                                               bias=nm[u % 2][:, br:br + 1], scale=SCALE,
                                               accum_out=den[:, u, br:br + 1])
                ins.then_inc(p_e, 1)

            def empty(i, u):
                after(act, pt, i * NU + u + 1)
                after(act, pv, i * NU + u - 1 if u else i * NU)
                n = width(u) // P
                nc.scalar.activation(PT[u % 2][:, 0, 0:n, :], pT[:, 0, 0:n, :], ACT.Copy).then_inc(pe_a, 1)

            with act.Fori(0, 2 * G) as i:
                exps(i, 0)
                after(act, c_sub, i + 1)
                nc.scalar.activation(cs[:], cs[:], ACT.Exp, scale=SCALE).then_inc(c_exp, 1)
                exps(i, 1)
                empty(i, 0)
                for u in range(NU):
                    if u + 2 < NU:
                        exps(i, u + 2)
                    if u + 1 < NU:
                        empty(i, u + 1)

        @block.vector
        def _(v):
            after(v, cn, 0)
            cm = keep["masks"][:, L_CM:L_CM + NQT * 32].rearrange("p (q n) -> p q n", q=NQT)
            cmf, cngf = (t.unsqueeze(1).to_broadcast([P, 2, NQT, 32]) for t in (cm, cneg[:]))
            nc.vector.tensor_scalar(cneg[:], cm, -NEG, NEG, ALU.mult, ALU.add).then_inc(cn, 1)
            nc.vector.memset(cs[:], 0.0).then_inc(cn, 1)
            after(v, cn, 2)

            def top(i, u):
                b, n, qt = u % 2, width(u), u % NQT
                after(v, s_p, i * NU + u + 1)
                diag = pS[b][:, :, qt * P:(qt + 1) * P]
                nc.vector.tensor_tensor(diag, diag, const[:, C_CAUS:C_CAUS + P].unsqueeze(1)
                                        .to_broadcast([P, 2, P]), ALU.add).then_inc(m_d, 1)
                after(v, m_d, i * NU + u + 1)
                nc.vector.tensor_reduce(mx[b][:], pS[b][:, :, 0:n], AX_X, ALU.max).then_inc(m_x, 1)
                after(v, m_x, i * NU + u + 1)
                nc.vector.tensor_scalar(nm[b][:], mx[b][:], -SCALE, None, ALU.mult).then_inc(nm_r, 1)

            def compressed_scores(i):
                s = cs[:]
                s3 = s.rearrange("p a q n -> p (a q) n")[:, :, 0:PCMP]
                after(v, c_s, i + 1)
                after(v, ct, i)
                for par in range(2):
                    ins = nc.vector.tensor_tensor(s[:, par, :, 0:PCMP],
                                                  (pC[:, 0:P] if par == 0 else pX[:, 0, :])
                                                  .rearrange("p (q n) -> p q n", q=NQT)[:, :, 0:PCMP],
                                                  cneg[:, :, 0:PCMP], ALU.add)
                ins.then_inc(c_add, 1)
                after(v, c_add, i + 1)
                nc.vector.tensor_reduce(cmx[:].rearrange("p a q -> p (a q)"), s3, AX_X, ALU.max).then_inc(c_max, 1)
                after(v, c_max, i + 1)
                nc.vector.tensor_tensor(s3, s3, cmx[:].rearrange("p a q -> p (a q)").unsqueeze(2)
                                        .to_broadcast([P, NU, PCMP]), ALU.subtract).then_inc(c_sub, 1)

            def compressed_weights(i):
                after(v, c_exp, i + 1)
                for par in range(2):
                    ins = nc.vector.tensor_tensor(cs[:, par], cs[:, par], cm, ALU.mult)
                ins.then_inc(c_mul, 1)
                after(v, c_mul, i + 1)
                nc.vector.tensor_reduce(cden[:].rearrange("p a q -> p (a q)"),
                                        cs[:].rearrange("p a q n -> p (a q) n")[:, :, 0:PCMP], AX_X,
                                        ALU.add).then_inc(c_sum, 1)
                after(v, c_sum, i + 1)
                nc.vector.tensor_scalar(cden[:], cden[:], 1.0, None, ALU.max).then_inc(c_top, 1)
                after(v, c_top, i + 1)
                nc.vector.reciprocal(crd[:], cden[:]).then_inc(c_rd, 1)

            def empty(i, u):
                after(v, pt, i * NU + u + 1)
                after(v, pv, i * NU + u - 1 if u else i * NU)
                n = width(u) // P
                nc.vector.tensor_copy(PT[u % 2][:, 1, 0:n, :], pT[:, 1, 0:n, :]).then_inc(pe_v, 1)

            def combine(i, head0, u):
                par, qt = divmod(u, NQT)
                k = i * NU + u + 1
                head = head0 + par * G
                gate = gN[:, qt, :].rearrange("p (n a) -> p n a", a=32)
                after(v, p_e, k)
                nc.vector.reciprocal(rd[:, 0:2], den[:, u, :]).then_inc(rd_a, 1)
                after(v, rd_a, k)
                after(v, c_rd, i + 1)
                nc.vector.tensor_tensor(rd[:, 2:3], crd[:, par, qt:qt + 1], gate[:, 0, bass.ds(head, 1)], ALU.mult)
                nc.vector.tensor_tensor(rd[:, 0:2].unsqueeze(2), rd[:, 0:2].unsqueeze(2),
                                        gate[:, 1:3, bass.ds(head, 1)], ALU.mult).then_inc(rd_b, 1)
                after(v, rd_b, k)
                after(v, pv, k)
                after(v, ot, i)
                o = lambda n: pC[:, 256 + DH * n:256 + DH * n + DH]
                nc.vector.tensor_scalar(acc[:, 0, :], o(0), rd[:, 0:1], None, ALU.mult).then_inc(a0, 1)
                after(v, a0, k)
                nc.vector.scalar_tensor_tensor(acc[:, 1, :], o(1), rd[:, 1:2], acc[:, 0, :], ALU.mult,
                                               ALU.add).then_inc(a1, 1)
                after(v, a1, k)
                nc.vector.scalar_tensor_tensor(oN[:, qt, par, :], o(2), rd[:, 2:3], acc[:, 1, :], ALU.mult,
                                               ALU.add).then_inc(a2, 1)
                after(v, a2, k)

            def step(hp, g):
                i = hp * G + g
                top(i, 0)
                compressed_scores(i)
                top(i, 1)
                compressed_weights(i)
                after(v, ct, i + 1)
                nc.vector.tensor_copy(PTc[0:PCMP].rearrange("p u n -> p (u n)"),
                                      pT[0:PCMP].rearrange("p a q n -> p (a q n)")).then_inc(ct_e, 1)
                empty(i, 0)
                for u in range(NU):
                    if u + 2 < NU:
                        top(i, u + 2)
                    if u + 1 < NU:
                        empty(i, u + 1)
                    combine(i, 2 * hp * G + g, u)
                after(v, ot, i + 1)
                nc.vector.tensor_tensor(oT[:, bass.ds(i + HG, 1), 0:SEQ].rearrange("p a t -> p (a t)"),
                                        pX[:].rearrange("p q t -> p (q t)"),
                                        hN[:, bass.ds(i + NG0, 1), 0:SEQ].rearrange("p a t -> p (a t)"),
                                        ALU.mult).then_inc(fin, 1)

            with v.Fori(0, 2) as hp:
                with v.Fori(0, G) as g:
                    step(hp, g)


def decode_phase(nc, io, keep):
    const, oT, gS, qS, ngS = (keep[n] for n in ("const", "oT", "gS", "qS", "ngS"))
    w1, w2p, w2v, hb = (keep[n] for n in ("w1", "w2p", "w2v", "hb"))
    R = KVH * G
    NSLC = (NSEL - 1) * SL + 1
    NT = NSEL // 2
    ident = const[:, C_ID:C_ID + P]
    cache = io["cache"]
    with ExitStack() as ctx:
        sb = lambda name, shape, dt=F32: ctx.enter_context(nc.sbuf_tensor(name, shape, dt))
        ps = lambda name, shape: ctx.enter_context(nc.psum_tensor(name, shape, F32))
        sem = _semaphores(nc, ctx, "d_")
        X = [[sb(f"X{k}{half}", [P, CD, KVH * DH]) for half in range(2)] for k in range(2)]
        XT = [sb(f"XT{n}", [P, CD // 2, 2, NSUB]) for n in range(2)]
        hs = [sb(f"hs{n}", [P, 2, NCMP]) for n in range(2)]
        kcT, vc = sb("kcT", [P, 2, NCMP]), sb("vc", [P, 2, KVH * DH])
        Kg, Vg = sb("Kg", [P, NT, KVH, DH]), sb("Vg", [P, NT, KVH, DH])
        Wt = sb("Wt", [P, WIN // P, 2 * KVH * DH])
        KgT = sb("KgT", [P, 2, NT * P])
        KwT = KgT[:, :, 0:WIN]
        qbd = sb("qbd", [P, 2, R])
        pg, pw, pn = sb("pg", [R, NT * P]), sb("pw", [R, WIN]), sb("pn", [R, 260])
        pc = pw[:, 0:256]
        PTc, PTg, PTw = sb("PTcd", [P, 2, R]), sb("PTg", [P, NT, R]), sb("PTw", [P, WIN // P, R])
        col = sb("col", [R, 16])
        acc, om = sb("acc", [R, KVH * DH]), sb("om", [R, KVH * DH])
        ohs = sb("ohs", [P, 2, G])
        i4, i16 = sb("i4", [R, NBLK]), sb("i16", [R, NBLK])
        sc, sc2 = sb("sc", [KVH, NBLK]), sb("sc2", [KVH, NBLK])
        top8, idx8 = sb("top8", [KVH, NSEL]), sb("idx8", [KVH, NSEL], U32)
        idxf, base = sb("idxf", [KVH, NSEL]), sb("base", [KVH, NSEL])
        rb = sb("rb", [KVH, NB, NBLK])
        rhs = sb("rhs", [KVH, 2, KVH, NT])
        gi = sb("gi", [P, 2 * KVH * NT], I32)
        pages = sb("pages", [KVH, NB * NPAGE], I32)
        tb = [ps(f"dtb{n}", [P, 512]) for n in range(2)]
        pH = [ps(f"dpH{n}", [P, 512]) for n in range(2)]
        pK, pO = ps("dpK", [P, 512]), ps("dpO", [P, 512])
        pS = ps("dpS", [P, 1024])
        oh = pg[0:KVH].rearrange("p (s j) -> p s j", s=NSEL)

        pages_in, passed = sem("pages_in"), sem("passed")
        x_in = [[sem(f"x_in{k}{half}") for half in range(2)] for k in range(2)]
        x_free = [sem("x_free0"), sem("x_free1")]
        w_in, w_out, new_in, g_in = sem("w_in"), sem("w_out"), sem("new_in"), sem("g_in")
        tr, ev = [sem("tr0"), sem("tr1")], [sem("ev0"), sem("ev1")]
        ct, cev = [sem("ct0"), sem("ct1")], [sem("cev0"), sem("cev1")]
        hid, sgm, hs_r = ([sem(f"{n}{b}") for b in range(2)] for n in ("hid", "sgm", "hs"))
        k2, k2_e = sem("k2"), sem("k2_e")
        init, bchain, cchain, rb_r = (sem(n) for n in ("init", "bchain", "cchain", "rb_r"))
        q_r, cs, nm_c, e_c, pn_r, ptc, ptc_e, pv_c, acc_r = (
            sem(n) for n in ("q_r", "cs", "nm_c", "e_c", "pn_r", "ptc", "ptc_e", "pv_c", "acc_r"))
        imp_r, imp, rhs_r, ix, gi_r = (sem(n) for n in ("imp_r", "imp", "rhs_r", "ix", "gi_r"))
        ss, nm_s, e_s, sw, nm_w, e_w = (sem(n) for n in ("ss", "nm_s", "e_s", "sw", "nm_w", "e_w"))
        pts, pts_e, ptw, ptw_e, pv_s, pv_w, om_r, omt, c_done = (
            sem(n) for n in ("pts", "pts_e", "ptw", "ptw_e", "pv_s", "pv_w", "om_r", "omt", "c_done"))
        leads = Leads(*x_free, w_out, c_done, *ev, *hid, *hs_r, k2_e, acc_r, gi_r, e_w)
        after = leads.after
        block = ctx.enter_context(nc.Block())
        ORDER = "H0 H1 K0 H2 K1 H3 C K2 K3 B".split()

        def plain(eng):
            eng.sem_inc(passed, 1)

        def steps(eng, do, at_c):
            def step(b, first=False, last=False):
                for item in ORDER:
                    if item == "C":
                        if not first:
                            at_c(b - 1)
                    else:
                        do(item, b, last)

            step(0, first=True)
            with eng.Fori(1, NB - 1) as b:
                step(b)
            step(NB - 1, last=True)
            at_c(NB - 1)

        def following(g, b, last):
            return (g + 1, b) if g < 3 else None if last else (0, b + 1)

        @block.sync
        def _(sp):
            sp.dma_start(pages[:], io["pages"].to_broadcast([KVH, NB * NPAGE])).then_inc(pages_in, 16)
            sp.wait_ge(pages_in, 16)

            def rows(b):
                for k in range(2):
                    after(sp, x_free[k], b)
                    plain(sp)
                    for half in range(2):
                        for n in range(NPAGE // 2):
                            page = sp.value_load(pages[0:1, bass.ds(b * NPAGE + (half * (NPAGE // 2) + n), 1)],
                                                 min_val=0, max_val=cache.shape[0] - 1)
                            sp.dma_start(X[k][half][n * 8:n * 8 + 8],
                                         cache[bass.ds(page, 1), :, k * KVH * DH:(k + 1) * KVH * DH]
                                         .rearrange("a (n j) e -> (a n) j e", j=CD)).then_inc(x_in[k][half], 16)

            def window(b):
                after(sp, c_done, b)
                after(sp, w_out, 16 * b)
                plain(sp)
                win = lambda a, n: io["win"][bass.ds(b, 1), 1 + 4 * a:1 + 4 * (a + n)].rearrange(
                    "a (p t) e -> p (a t) e", p=n)
                new = lambda a, n: io["new_rows"][bass.ds(b, 1), a:a + n]
                sp.dma_start(Wt[0:112], win(0, 112)).then_inc(w_in, 16)
                sp.dma_start(Wt[112:127], win(112, 15)).then_inc(w_in, 16)
                sp.dma_start(Wt[127:128, 0:3], io["win"][bass.ds(b, 1), 509:512]).then_inc(w_in, 16)
                sp.dma_start(Wt[127:128, 3], new(1024, 512)).then_inc(w_in, 16)
                for t, a in ((Kg, 512), (Vg, 768)):
                    sp.dma_start(t[SL:SL + 1, NT - 1].rearrange("p h d -> p (h d)"), new(a, 256)).then_inc(new_in, 16)
                sp.wait_ge(w_in, 64 * b + 64)
                plain(sp)
                sp.dma_start(io["win_sample"][bass.ds(b, 1)].rearrange("a (p t) e -> p (a t) e", p=P),
                             Wt[:]).then_inc(w_out, 16)

            rows(0)
            with sp.Fori(1, NB) as b:
                rows(b)
                window(b - 1)
            window(NB - 1)
            after(sp, w_out, 16 * NB)

        @block.gpsimd
        def _(pool):
            leads.give(pool)
            table = cache.rearrange("g r (s d) -> (g r s) d", d=DH)
            nc.gpsimd.memset(qbd[:], 0.0).then_inc(init, 1)
            nc.gpsimd.memset(pn[:], 0.0).then_inc(init, 1)
            nc.gpsimd.memset(sc[:], FORCED).then_inc(init, 1)
            with pool.Fori(0, NB) as b:
                after(pool, gi_r, b + 1)
                after(pool, c_done, b)
                plain(pool)
                for kind, tile in enumerate((Kg, Vg)):
                    for h in range(KVH):
                        for t in range(NT):
                            n = P if t < NT - 1 else SL
                            a = (kind * KVH + h) * NT + t
                            pool.indirect_dma_start(
                                out=tile[0:n, t, h, :], out_offset=None, in_=table,
                                in_offset=bass.IndirectOffsetOnAxis(ap=gi[0:n, a:a + 1], axis=0),
                            ).then_inc(g_in, 16)

        @block.tensor
        def _(pe):
            def turn(g, b, u):
                k, hp = divmod(g, 2)
                half, jq = u // 4, u % 4
                if jq == 0:
                    pe.wait_ge(x_in[k][half], 256 * b + 256)
                after(pe, ev[u % 2], 16 * b + 4 * g + u // 2)
                for j in range(4):
                    mm = nc.tensor.transpose(tb[u % 2][:, j * P:(j + 1) * P],
                                             X[k][half][:, 4 * jq + j, hp * P:(hp + 1) * P], ident)
                mm.then_inc(tr[u % 2], 1)
                if hp == 1 and u == 7:
                    pe.wait_ge(tr[1], 16 * b + 4 * g + 4)
                    pe.sem_inc(x_free[k], 1)

            def hidden(g, b, last):
                for n in range(2):
                    after(pe, ev[n], 16 * b + 4 * g + 4)
                after(pe, hs_r[g % 2], 2 * b + g // 2)
                then = following(g, b, last)
                for n in range(CL // 2):
                    r, jp = divmod(n, CD // 2)
                    mm = nc.tensor.matmul(pH[g % 2][:, 0:2 * NCMP], w1[:, g // 2, n, :],
                                          XT[g % 2][:, jp, :, r:r + NCMP],
                                          start=(n == 0), stop=(n == CL // 2 - 1))
                    if n == CL // 2 - 1:
                        mm.then_inc(hid[g % 2], 1)
                    if n % 2 == 0 and then:
                        turn(*then, n // 2)
                if g == 3:
                    for n in range(2):
                        after(pe, ev[n], 16 * b + (16 if last else 20))

            def second(g, b):
                after(pe, hs_r[g % 2], 2 * b + g // 2 + 1)
                after(pe, k2_e, 4 * b + g)
                after(pe, gi_r, b)
                h = hs[g % 2]
                if g < 2:
                    for par in range(2):
                        mm = nc.tensor.matmul(pK[:, 0:NCMP], w2p[:, par, :], h[:, par, :],
                                              start=(par == 0), stop=(par == 1))
                else:
                    for nt in range(2):
                        for par in range(2):
                            n = min(P, NCMP - nt * P)
                            mm = nc.tensor.matmul(pK[0:n, (2 * nt + par) * DH:(2 * nt + par + 1) * DH],
                                                  h[:, par, nt * P:nt * P + n], w2v[:, 1, :],
                                                  start=True, stop=True)
                mm.then_inc(k2, 1)

            def scores(out, keys, n, a=0):
                for hp in range(2):
                    mm = nc.tensor.matmul(out[0:R, a:a + n], qbd[:, hp, :], keys[:, hp, a:a + n],
                                          start=(hp == 0), stop=(hp == 1))
                return mm

            def chosen(b):
                pe.wait_ge(g_in, 1024 * b + 1024)
                pe.wait_ge(new_in, 32 * b + 32)
                units = [(Kg, hp, tq) for hp in range(2) for tq in range(2)] + [(Wt, hp, 0) for hp in range(2)]
                for u, (src, hp, tq) in enumerate(units):
                    if u >= 2:
                        pe.wait_ge(cev[u % 2], 3 * b + u // 2)
                    if u == 4:
                        pe.wait_ge(cev[1], 3 * b + 2)
                        scores(pS, KgT, 512)
                        scores(pS, KgT, NSLC - 512, 512).then_inc(ss, 1)
                        pe.wait_ge(w_in, 64 * b + 64)
                    for j in range(4):
                        t = 4 * tq + j
                        n = SL + 1 if src is Kg and t == NT - 1 else P
                        rows = (Kg[0:n, t, 2 * hp:2 * hp + 2, :].rearrange("p h d -> p (h d)") if src is Kg
                                else Wt[:, t, hp * P:(hp + 1) * P])
                        mm = nc.tensor.transpose(tb[u % 2][:, j * P:j * P + n], rows, ident[0:n, 0:n])
                    mm.then_inc(ct[u % 2], 1)
                for n in range(2):
                    pe.wait_ge(cev[n], 3 * b + 3)
                pe.wait_ge(e_s, b + 1)
                scores(pS, KwT, WIN).then_inc(sw, 1)
                plain(pe)
                for t in range(NT):
                    n = min(P, NSLC - t * P)
                    mm = nc.tensor.transpose(tb[0][0:n, t * R:(t + 1) * R], pg[:, t * P:t * P + n], ident[0:R, 0:R])
                mm.then_inc(pts, 1)
                pe.wait_ge(pts_e, b + 1)
                after(pe, acc_r, b + 1)
                for t in range(NT):
                    n = min(P, NSLC - t * P)
                    mm = nc.tensor.matmul(pO[0:R, 0:256], PTg[0:n, t, :], Vg[0:n, t].rearrange("p h d -> p (h d)"),
                                          start=(t == 0), stop=(t == NT - 1))
                mm.then_inc(pv_s, 1)
                after(pe, e_w, b + 1)
                plain(pe)
                for t in range(WIN // P):
                    mm = nc.tensor.transpose(tb[1][:, t * R:(t + 1) * R], pw[:, t * P:(t + 1) * P], ident[0:R, 0:R])
                mm.then_inc(ptw, 1)
                pe.wait_ge(ptw_e, b + 1)
                for t in range(WIN // P):
                    mm = nc.tensor.matmul(pO[0:R, 256:512], PTw[:, t, :], Wt[:, t, 256:512],
                                          start=(t == 0), stop=(t == WIN // P - 1))
                mm.then_inc(pv_w, 1)
                pe.wait_ge(om_r, b + 1)
                plain(pe)
                for hp in range(2):
                    mm = nc.tensor.transpose(tb[0][:, hp * R:(hp + 1) * R], om[:, hp * P:(hp + 1) * P],
                                             ident[0:R, 0:R])
                mm.then_inc(omt, 1)
                after(pe, c_done, b + 1)

            def blocks(b):
                after(pe, k2_e, 4 * b + 4)
                pe.wait_ge(q_r, b + 1)
                scores(pS, kcT, NCMP).then_inc(cs, 1)
                pe.wait_ge(pn_r, b + 1)
                plain(pe)
                for nt in range(2):
                    n = min(P, NCMP - nt * P)
                    mm = nc.tensor.transpose(tb[0][0:n, nt * R:(nt + 1) * R], pn[:, 1 + nt * P:1 + nt * P + n],
                                             ident[0:R, 0:R])
                mm.then_inc(ptc, 1)
                pe.wait_ge(imp_r, b + 1)
                plain(pe)
                nc.tensor.matmul(pK[0:KVH, 0:NBLK], const[0:R, C_GRP:C_GRP + KVH], i16[:],
                                 start=True, stop=True).then_inc(imp, 1)
                pe.wait_ge(ptc_e, b + 1)
                for nt in range(2):
                    n = min(P, NCMP - nt * P)
                    mm = nc.tensor.matmul(pO[0:R, 0:256], PTc[0:n, nt, :], vc[0:n, nt, :],
                                          start=(nt == 0), stop=(nt == 1))
                mm.then_inc(pv_c, 1)
                pe.wait_ge(rhs_r, b + 1)
                plain(pe)
                for a in range(2):
                    mm = nc.tensor.matmul(pK[:, 128:128 + KVH * NT], const[0:KVH, C_HALF + a * P:C_HALF + (a + 1) * P],
                                          rhs[:, a].rearrange("p h t -> p (h t)"), start=(a == 0), stop=(a == 1))
                mm.then_inc(ix, 1)
                after(pe, gi_r, b + 1)

            def do(item, b, last):
                if item == "B":
                    blocks(b)
                elif item[0] == "H":
                    hidden(int(item[1]), b, last)
                else:
                    second(int(item[1]), b)

            pe.wait_ge(init, 3)
            for u in range(8):
                turn(0, 0, u)
            steps(pe, do, chosen)

        def empty(eng, g, b):
            n = 0 if eng is nc.vector else 1
            after(eng, hid[g % 2], 2 * b + g // 2)
            for u in range(n, 8, 2):
                half, jq = u // 4, u % 4
                eng.wait_ge(tr[n], 16 * b + 4 * g + u // 2 + 1)
                src = tb[n][:].rearrange("p (j a s) -> p a j s", j=2, a=2)
                for par in range(2):
                    for a in range(2):
                        dst = XT[g % 2][a * DH:(a + 1) * DH, 2 * jq:2 * jq + 2, par, half * P:(half + 1) * P]
                        s = src[par * DH:(par + 1) * DH, a]
                        ins = (nc.vector.tensor_copy(dst, s) if n == 0 else
                               nc.scalar.activation(dst, s, ACT.Copy))
                ins.then_inc(ev[n], 1)

        def empty_chosen(eng, b):
            n = 0 if eng is nc.vector else 1
            units = [(KgT, hp, tq) for hp in range(2) for tq in range(2)] + [(KwT, hp, 0) for hp in range(2)]
            for u in range(n, 6, 2):
                dst, hp, tq = units[u]
                eng.wait_ge(ct[n], 3 * b + u // 2 + 1)
                if u >= 4:
                    eng.wait_ge(ss, b + 1)
                m = 512 if u >= 4 or tq == 0 else NSLC - 512
                dst = dst[:, hp, tq * 512:tq * 512 + m]
                if n == 0:
                    nc.vector.tensor_copy(dst, tb[0][:, 0:m]).then_inc(cev[0], 1)
                else:
                    nc.scalar.activation(dst, tb[1][:, 0:m], ACT.Copy).then_inc(cev[1], 1)

        @block.scalar
        def _(act):
            def sigmoid(g, b):
                after(act, hid[g % 2], 2 * b + g // 2 + 1)
                after(act, k2_e, 4 * b + max(g - 1, 0))
                nc.scalar.activation(hs[g % 2][:].rearrange("p a n -> p (a n)"), pH[g % 2][:, 0:2 * NCMP],
                                     ACT.Sigmoid, bias=hb[:, g // 2:g // 2 + 1]).then_inc(sgm[g % 2], 1)

            def chosen(b):
                empty_chosen(nc.scalar, b)
                act.wait_ge(nm_s, b + 1)
                nc.scalar.activation(pg[:, 0:NSLC], pS[0:R, 0:NSLC], ACT.Exp, bias=col[:, 4:5], scale=SCALE,
                                     accum_out=col[:, 5:6]).then_inc(e_s, 1)
                act.wait_ge(nm_w, b + 1)
                nc.scalar.activation(pw[:], pS[0:R, 0:WIN], ACT.Exp, bias=col[:, 8:9], scale=SCALE,
                                     accum_out=col[:, 9:10]).then_inc(e_w, 1)

            def do(item, b, last):
                if item[0] == "H":
                    g = int(item[1])
                    then = following(g, b, last)
                    if then:
                        empty(nc.scalar, *then)
                    sigmoid(g, b)
                elif item == "B":
                    act.wait_ge(nm_c, b + 1)
                    nc.scalar.activation(pc[:, 0:NCMP], pS[0:R, 0:NCMP], ACT.Exp, bias=col[:, 1:2], scale=SCALE,
                                         accum_out=col[:, 2:3]).then_inc(e_c, 1)

            empty(nc.scalar, 0, 0)
            steps(act, do, chosen)

        @block.vector
        def _(v):
            V = nc.vector

            def hidden(g, b):
                v.wait_ge(sgm[g % 2], 2 * b + g // 2 + 1)
                V.scalar_tensor_tensor(hs[g % 2][:].rearrange("p a n -> p (a n)"), pH[g % 2][:, 0:2 * NCMP],
                                       hb[:, g // 2:g // 2 + 1], hs[g % 2][:].rearrange("p a n -> p (a n)"),
                                       ALU.add, ALU.mult).then_inc(hs_r[g % 2], 1)

            def second(g, b):
                v.wait_ge(k2, 4 * b + g + 1)
                if g < 2:
                    V.tensor_copy(kcT[:, g, :], pK[:, 0:NCMP]).then_inc(k2_e, 1)
                else:
                    cols = slice((g - 2) * P, (g - 1) * P)
                    V.tensor_copy(vc[:, 0, cols], pK[:, 0:P])
                    V.tensor_copy(vc[0:NCMP - P, 1, cols], pK[0:NCMP - P, P:2 * P]).then_inc(k2_e, 1)

            def queries(b):
                for hp in range(2):
                    for par in range(2):
                        rows = slice(par * DH, (par + 1) * DH)
                        a = hp * 2 * G + par * G
                        ins = V.tensor_copy(qbd[rows, hp, a:a + G].unsqueeze(2),
                                            qS[rows, hp * G:(hp + 1) * G, bass.ds(b, 1)])
                ins.then_inc(q_r, 1)

            def chosen(b):
                c = Chain(v, cchain, b, 10)
                empty_chosen(V, b)
                v.wait_ge(ss, b + 1)
                c(V.tensor_reduce(col[:, 3:4], pS[0:R, 0:NSLC], AX_X, ALU.max))
                V.tensor_scalar(col[:, 4:5], col[:, 3:4], -SCALE, None, ALU.mult).then_inc(nm_s, 1)
                v.wait_ge(sw, b + 1)
                c(V.tensor_reduce(col[:, 7:8], pS[0:R, 0:WIN], AX_X, ALU.max))
                V.tensor_scalar(col[:, 8:9], col[:, 7:8], -SCALE, None, ALU.mult).then_inc(nm_w, 1)
                v.wait_ge(pts, b + 1)
                V.tensor_copy(PTg[:, 0:NT - 1, :], tb[0][:, 0:(NT - 1) * R].rearrange("p (t r) -> p t r", r=R))
                V.tensor_copy(PTg[0:SL + 1, NT - 1, :], tb[0][0:SL + 1, (NT - 1) * R:NT * R]).then_inc(pts_e, 1)
                v.wait_ge(ptw, b + 1)
                V.tensor_copy(PTw[:], tb[1][:, 0:WIN // P * R].rearrange("p (t r) -> p t r", r=R)).then_inc(ptw_e, 1)
                v.wait_ge(e_s, b + 1)
                after(v, e_w, b + 1)
                c(V.reciprocal(col[:, 5:6], col[:, 5:6]))
                c(V.reciprocal(col[:, 9:10], col[:, 9:10]))
                c(V.tensor_tensor(col[:, 5:6], col[:, 5:6], gS[:, 1, bass.ds(b, 1)], ALU.mult))
                c(V.tensor_tensor(col[:, 9:10], col[:, 9:10], gS[:, 2, bass.ds(b, 1)], ALU.mult))
                v.wait_ge(pv_s, b + 1)
                v.wait_ge(pv_w, b + 1)
                c(V.scalar_tensor_tensor(om[:], pO[0:R, 0:256], col[:, 5:6], acc[:], ALU.mult, ALU.add))
                c(V.scalar_tensor_tensor(om[:], pO[0:R, 256:512], col[:, 9:10], om[:], ALU.mult, ALU.add))
                V.tensor_tensor(om[:], om[:], const[0:R, C_OWN:C_OWN + 256], ALU.mult).then_inc(om_r, 1)
                v.wait_ge(omt, b + 1)
                for hp in range(2):
                    a = hp * R + hp * 2 * G
                    pair = tb[0][:, a:a + 2 * G].rearrange("p (a g) -> p g a", a=2)
                    c(V.tensor_reduce(ohs[:, hp, :], pair, AX_X, ALU.add))
                c.end()
                V.tensor_tensor(oT[:, HG:2 * HG, bass.ds(b + SEQ, 1)], ohs[:].rearrange("p a g -> p (a g)").unsqueeze(2),
                                ngS[:, :, bass.ds(b, 1)], ALU.mult).then_inc(c_done, 1)

            def blocks(b):
                c = Chain(v, bchain, b, 13, plain)
                v.wait_ge(cs, b + 1)
                c(V.tensor_reduce(col[:, 0:1], pS[0:R, 0:NCMP], AX_X, ALU.max))
                V.tensor_scalar(col[:, 1:2], col[:, 0:1], -SCALE, None, ALU.mult).then_inc(nm_c, 1)
                v.wait_ge(e_c, b + 1)
                c(V.reciprocal(col[:, 2:3], col[:, 2:3]))
                V.tensor_scalar(pn[:, 1:1 + NCMP], pc[:, 0:NCMP], col[:, 2:3], None, ALU.mult).then_inc(pn_r, 1)
                v.wait_ge(pn_r, b + 1)
                c(V.tensor_reduce(i4[:], pn[:, 0:4 * NBLK].rearrange("p (j a) -> p j a", a=4), AX_X, ALU.add))
                V.tensor_tensor(i16[:].unsqueeze(2), i4[:].unsqueeze(2),
                                pn[:, 4:4 + 4 * NBLK].rearrange("p (j a) -> p j a", a=4)[:, :, 0:1],
                                ALU.add).then_inc(imp_r, 1)
                v.wait_ge(ptc, b + 1)
                V.tensor_copy(PTc[:, 0, :], tb[0][:, 0:R])
                V.tensor_copy(PTc[0:NCMP - P, 1, :], tb[0][0:NCMP - P, R:2 * R]).then_inc(ptc_e, 1)
                v.wait_ge(imp, b + 1)
                c(V.tensor_copy(sc[:, 1:NBLK - 1], pK[0:KVH, 1:NBLK - 1]), True)
                c(V.max(top8[:, 0:8], sc[:]), True)
                c(V.match_replace(sc2[:], top8[:, 0:8], sc[:], -1.0), True)
                c(V.max_index(idx8[:, 0:8], top8[:, 0:8], sc[:]), True)
                c(V.max(top8[:, 8:16], sc2[:]), True)
                c(V.max_index(idx8[:, 8:16], top8[:, 8:16], sc2[:]))
                c(V.tensor_copy(idxf[:], idx8[:]))
                c(V.tensor_tensor(oh, const[0:KVH, C_SLOT:C_SLOT + NBLK].unsqueeze(1).to_broadcast([KVH, NSEL, NBLK]),
                                  idxf[:].unsqueeze(2).to_broadcast([KVH, NSEL, NBLK]), ALU.is_equal))
                c(V.tensor_tensor(oh, oh, rb[:, bass.ds(b, 1), :].to_broadcast([KVH, NSEL, NBLK]), ALU.mult))
                c(V.tensor_reduce(base[:], oh, AX_X, ALU.add))
                for a in range(2):
                    half = base[:].rearrange("p (t a) -> p a t", a=2)[:, a:a + 1, :]
                    ins = V.tensor_tensor(rhs[:, a], half.to_broadcast([KVH, KVH, NT]),
                                          const[0:KVH, C_EXP:C_EXP + 32].rearrange("p (h t) -> p h t", t=NT),
                                          ALU.mult)
                ins.then_inc(rhs_r, 1)
                v.wait_ge(pv_c, b + 1)
                V.tensor_scalar(acc[:], pO[0:R, 0:256], gS[:, 0, bass.ds(b, 1)], None, ALU.mult).then_inc(acc_r, 1)
                v.wait_ge(ix, b + 1)
                V.tensor_tensor(gi[:].rearrange("p (a n) -> p a n", a=2),
                                pK[:, 128:128 + KVH * NT].unsqueeze(1).to_broadcast([P, 2, KVH * NT]),
                                const[:, C_ROW:C_ROW + 64].rearrange("p (a n) -> p a n", a=2),
                                ALU.add).then_inc(gi_r, 1)
                c.end()

            def do(item, b, last):
                g = int(item[1]) if len(item) > 1 else None
                if item[0] == "H":
                    then = following(g, b, last)
                    if then:
                        empty(V, *then)
                    hidden(g, b)
                elif item[0] == "K":
                    second(g, b)
                else:
                    queries(b)
                    blocks(b)

            v.wait_ge(pages_in, 16)
            v.wait_ge(init, 3)
            r3 = rb[:].rearrange("p b (g a) -> p (b g) a", a=2)
            for a in range(2):
                ins = V.tensor_scalar(r3[:, :, a:a + 1], pages[:].unsqueeze(2), float(PAGE), float(SL * a),
                                      ALU.mult, ALU.add)
            ins.then_inc(rb_r, 1)
            v.wait_ge(rb_r, 1)
            empty(V, 0, 0)
            steps(v, do, chosen)


def output_phase(nc, io, keep):
    const, oT = keep["const"], keep["oT"]
    NC = D // 512
    tiles = [(t * P, P) for t in range(NQT)] + [(SEQ, NB)]
    with ExitStack() as ctx:
        sb = lambda name, shape, dt=F32: ctx.enter_context(nc.sbuf_tensor(name, shape, dt))
        sem = _semaphores(nc, ctx, "o_")
        w = [sb(f"wo{n}", [P, KT, 512]) for n in range(2)]
        z = [sb(f"z{n}", [P, D]) for n in range(len(tiles))]
        gb = sb("gb", [P, 2, D])
        st = sb("stat", [P, len(tiles), 4])
        junk = sb("junk", [P, 512])
        bank = [ctx.enter_context(nc.psum_tensor(f"py{n}", [P, 512], F32)) for n in range(8)]
        w_in = [sem("w_in0"), sem("w_in1")]
        x_in, gb_in, y_out = sem("x_in"), sem("gb_in"), sem("y_out")
        mm_r, add_r = sem("mm"), sem("add")
        s0, s1, s2, s3, s4, s5, s6, s7 = (sem(f"s{n}") for n in range(8))
        nt = len(tiles)
        block = ctx.enter_context(nc.Block())

        @block.sync
        def _(sp):
            def load(c):
                sp.dma_start(w[c % 2][:], io["w_out"][c]).then_inc(w_in[c % 2], 16)
            load(0)
            for n, (t0, m) in enumerate(tiles):
                sp.dma_start(z[n][0:m], io["x"][t0:t0 + m]).then_inc(x_in, 16)
            load(1)
            sp.dma_start(gb[:], io["ln"].unsqueeze(0).to_broadcast([P, 2, D])).then_inc(gb_in, 16)
            for c in range(2, NC):
                sp.wait_ge(mm_r, nt * (c - 1))
                load(c)
            for n, (t0, m) in enumerate(tiles):
                sp.wait_ge(s7, n + 1)
                sp.dma_start(io["y"][t0:t0 + m], z[n][0:m]).then_inc(y_out, 16)
            sp.wait_ge(y_out, 16 * nt)

        @block.tensor
        def _(pe):
            for c in range(NC):
                pe.wait_ge(w_in[c % 2], 16 * (c // 2 + 1))
                for n, (t0, m) in enumerate(tiles):
                    s = c * nt + n
                    if s >= 8:
                        pe.wait_ge(add_r, s - 7)
                    for k in range(KT):
                        mm = nc.tensor.matmul(bank[s % 8][0:m, :], oT[:, k, t0:t0 + m], w[c % 2][:, k, :],
                                              start=(k == 0), stop=(k == KT - 1))
                    mm.then_inc(mm_r, 1)

        @block.scalar
        def _(act):
            for n, (t0, m) in enumerate(tiles):
                act.wait_ge(s2, n + 1)
                if n:
                    act.wait_ge(s3, n)
                sq = [bank[(n % 2) * 4 + c] for c in range(NC)]
                for c in range(NC):
                    ins = nc.scalar.activation(sq[c][0:m, :], z[n][0:m, c * 512:(c + 1) * 512], ACT.Square,
                                               accum_out=st[0:m, n, c:c + 1])
                ins.then_inc(s3, 1)
                act.wait_ge(s4, n + 1)
                nc.scalar.activation(st[0:m, n, 1:2], st[0:m, n, 0:1], ACT.Ln, scale=1.0 / D,
                                     bias=const[0:m, C_EPS + 1:C_EPS + 2]).then_inc(s5, 1)
                act.wait_ge(s5, 2 * n + 1)
                nc.scalar.activation(st[0:m, n, 2:3], st[0:m, n, 1:2], ACT.Exp, scale=-0.5).then_inc(s5, 1)

        @block.vector
        def _(v):
            v.wait_ge(x_in, 16 * nt)
            v.wait_ge(gb_in, 16)
            V = nc.vector
            def norm(n, m):
                zz = z[n][0:m]
                v.wait_ge(add_r, (NC - 1) * nt + n + 1)
                V.tensor_reduce(st[0:m, n, 0:1], zz, AX_X, ALU.add).then_inc(s0, 1)
                v.wait_ge(s0, n + 1)
                V.tensor_scalar(st[0:m, n, 1:2], st[0:m, n, 0:1], 1.0 / D, None, ALU.mult).then_inc(s1, 1)
                v.wait_ge(s1, n + 1)
                V.tensor_scalar(zz, zz, st[0:m, n, 1:2], None, ALU.subtract).then_inc(s2, 1)

            def scale(n, m):
                zz = z[n][0:m]
                v.wait_ge(s3, n + 1)
                V.tensor_reduce(st[0:m, n, 0:1], st[0:m, n, 0:4], AX_X, ALU.add).then_inc(s4, 1)
                v.wait_ge(s5, 2 * n + 2)
                V.scalar_tensor_tensor(zz, zz, st[0:m, n, 2:3], gb[0:m, 0], ALU.mult, ALU.mult).then_inc(s6, 1)
                v.wait_ge(s6, n + 1)
                V.tensor_tensor(zz, zz, gb[0:m, 1], ALU.add).then_inc(s7, 1)

            for c in range(NC):
                for n, (t0, m) in enumerate(tiles):
                    s = c * nt + n
                    v.wait_ge(mm_r, s + 1)
                    part = z[n][0:m, c * 512:(c + 1) * 512]
                    V.scalar_tensor_tensor(part, part, ALPHA, bank[s % 8][0:m, :], ALU.mult,
                                           ALU.add).then_inc(add_r, 1)
            norm(0, tiles[0][1])
            for n in range(nt):
                if n + 1 < nt:
                    norm(n + 1, tiles[n + 1][1])
                scale(n, tiles[n][1])


def build(nc, io):
    with ExitStack() as ctx:
        def tile(stack, name, shape):
            keep[name] = stack.enter_context(nc.sbuf_tensor(name, shape, F32))
            return keep[name]

        keep = {}
        tile(ctx, "const", [P, C_N])
        tile(ctx, "oT", [P, KT, T])
        tile(ctx, "gS", [16, 3, NB])
        tile(ctx, "qS", [P, NQ, NB])
        tile(ctx, "ngS", [P, NG, NB])
        tile(ctx, "w1", [P, 2, CL // 2, 2 * DH])
        tile(ctx, "w2v", [P, 2, DH])
        tile(ctx, "w2p", [P, 2, P])
        tile(ctx, "hb", [P, 2])
        with ExitStack() as early:
            tile(early, "masks", [P, L_N])
            xT = tile(early, "xT", [P, KT, T])
            strips = tile(early, "strips", [P, 2, KT, P])
            keep["w"] = [strips[:, n] for n in range(2)]
            hgrn_phase(nc, io, keep)
            tile(early, "hN", [P, NSTRIP, T])
            projection_phase(nc, io, keep)
            keep["NV"] = xT[:].rearrange("p k t -> p (k t)")[:, 0:NQT * 1536].rearrange("p (c e) -> p c e", c=NQT)
            tile(early, "gN", [P, NQT, P])
            tile(early, "kcT_p", [P, 2, PCMP])
            tile(early, "vc_p", [32, KVH * DH])
            rows_phase(nc, io, keep)
            prompt_phase(nc, io, keep)
        decode_phase(nc, io, keep)
        output_phase(nc, io, keep)


def _columns():
    d = np.arange(P)
    hq0, hf0, hi0, hg0, nq0 = (n * HG * P for n in range(5))
    kv0 = nq0 + KVH * G * DH
    bg0 = kv0 + 6 * KVH * DH
    ng0 = bg0 + NW
    strips = [c + h * P + d for h in range(HG) for c in (hf0, hi0, hq0, hg0)]
    own = [((2 * hp + d // DH) * G + g) * DH + d % DH for hp in range(2) for g in range(G)]
    strips += [nq0 + o for o in own]
    strips += [kv0 + s * P + d for s in range(NKV)]
    strips += [ng0 + o for o in own]
    strips.append(np.where(d % 32 < KVH * G, np.minimum(bg0 + d // 32 * KVH * G + d % 32, bg0 + NW - 1), -1))
    return strips, own


def kernel(x_prompt, x_sample, cache_kv, cache_win, state_hgrn, page_table, w_in, hg_lb, hg_norm_g,
           cmp_w1, cmp_w2, cmp_pe, w_out, ln_g, ln_b):
    import concourse.bacc as bacc
    from concourse.bass_utils import run_bass_kernel_spmd

    f = lambda a: np.asarray(a)
    x = np.concatenate([f(x_prompt)[0], f(x_sample)[:, 0]], 0)
    strips, own = _columns()
    wi = f(w_in)[0].reshape(KT, P, -1)
    wi = np.concatenate([wi, np.zeros((KT, P, 1), np.float32)], 2)
    ws = np.stack([wi[:, :, s].transpose(1, 0, 2) for s in strips])
    rows = np.concatenate([np.arange(HG * P)] + [HG * P + o for o in own])
    wo = f(w_out)[0][rows].reshape(KT, P, 4, 512).transpose(2, 1, 0, 3)
    arrays = {
        "const": _constants(),
        "masks": _prompt_constants(),
        "xT": x.T.reshape(KT, P, T).transpose(1, 0, 2),
        "x": x,
        "w_in": ws,
        "hg_lb": f(hg_lb).reshape(2, HG, P).transpose(2, 0, 1),
        "norm_g": f(hg_norm_g)[0].reshape(HG, P).T,
        "state": f(state_hgrn)[0],
        "cache": f(cache_kv)[0].reshape(-1, PAGE, 4 * KVH * DH),
        "win": f(cache_win)[0].reshape(NB, WIN, 2 * KVH * DH),
        "pages": f(page_table).reshape(1, NB * NPAGE),
        "w1": f(cmp_w1)[0].reshape(2, CL // 2, 2 * DH, 2 * DH).transpose(2, 0, 1, 3),
        "w2": f(cmp_w2)[0].transpose(1, 0, 2),
        "pe": f(cmp_pe)[0].reshape(2, CL // 2, 2 * DH).transpose(2, 0, 1),
        "w_out": wo,
        "ln": np.concatenate([f(ln_g), f(ln_b)], 0),
    }
    outs = {
        "y": (T, D), "kv_prompt": (SEQ, 4 * KVH * DH), "win_prompt": (SEQ, 2 * KVH * DH),
        "hgrn_prompt": (HG, P, P), "kv_sample": (NB, 4 * KVH * DH), "win_sample": (NB, WIN, 2 * KVH * DH),
        "hgrn_sample": (NB, HG, P, P),
    }
    nc = bacc.Bacc("TRN2", target_bir_lowering=False, num_devices=1)
    arrays = {n: np.ascontiguousarray(a) for n, a in arrays.items()}
    io = {n: nc.dram_tensor("d_" + n, a.shape, mybir.dt.from_np(a.dtype), kind="ExternalInput").ap()
          for n, a in arrays.items()}
    io |= {n: nc.dram_tensor("d_" + n, s, F32, kind="ExternalOutput").ap() for n, s in outs.items()}
    io["new_rows"] = nc.dram_tensor("new_rows", (NB, 6 * KVH * DH), F32, kind="Internal").ap()
    build(nc, io)
    got = run_bass_kernel_spmd(nc, [{"d_" + n: a for n, a in arrays.items()}], core_ids=[0]).results[0]
    r = {n: got["d_" + n] for n in outs}
    y = r["y"]
    return (y[None, :SEQ], y[SEQ:, None], r["kv_prompt"].reshape(1, 1, SEQ, 4, KVH, DH),
            r["win_prompt"].reshape(1, 1, WIN, 2, KVH, DH), r["hgrn_prompt"][None, None],
            r["kv_sample"].reshape(1, NB, 1, 4, KVH, DH), r["win_sample"].reshape(1, NB, WIN, 2, KVH, DH),
            r["hgrn_sample"][None])
```
